# Optimizing a Trainium2 kernel written in Bass

```python
import jax, jax.numpy as jnp
from jax import lax
import numpy as np
import math

D_MODEL = 1024
BATCH = 1
SEQ = 512
DEPTH = 1

CHUNK = 64
N_META = 16
EPS = 1e-6

D_MIX = D_MODEL
M_HEADS = 4
M_HEAD_DIM = (D_MIX // 2) // M_HEADS
M_WIDTH = M_HEADS * M_HEAD_DIM
CONV_W = 4
F_HEADS = 8
F_HEAD_DIM = (D_MIX - M_WIDTH) // F_HEADS
F_WIDTH = F_HEADS * F_HEAD_DIM
Q_BLOCK = 128

PROJ_SIZES = (M_WIDTH, M_WIDTH, M_WIDTH, M_WIDTH, M_HEADS, M_HEADS, F_WIDTH, F_WIDTH, F_WIDTH, F_HEADS)
PROJ_DIM = 4 * M_WIDTH + 2 * M_HEADS + 3 * F_WIDTH + F_HEADS

PEER_HEADS = 8
N_KEYS = 128
N_EXPERTS = N_KEYS * N_KEYS
PEER_TOPK = 16
PEER_QDIM = 256
PEER_HALF = PEER_QDIM // 2
PEER_TOKEN_BLOCK = 128


def _rmsnorm(x, g):
    xf = x.astype(jnp.float32)
    y = xf * lax.rsqrt(jnp.mean(xf * xf, axis=-1, keepdims=True) + EPS)
    return (y * g.astype(jnp.float32)).astype(x.dtype)

def _proj_splits():
    out, acc = [], 0
    for s in PROJ_SIZES[:-1]:
        acc += s
        out.append(acc)
    return out

def _causal_dwconv(x, w):
    c = x.shape[-1]
    return lax.conv_general_dilated(
        x, w.astype(x.dtype)[:, None, :], window_strides=(1,),
        padding=[(CONV_W - 1, 0)], dimension_numbers=("NWC", "WIO", "NWC"),
        feature_group_count=c)

def _mlstm(q, k, v, o_pre, i_pre, f_pre, out_gain):
    f32 = jnp.float32
    B, L, _ = q.shape
    n_chunks = -(-L // CHUNK)
    pad = n_chunks * CHUNK - L

    def heads(t):
        t = jnp.pad(t.astype(f32), ((0, 0), (0, pad), (0, 0)))
        return t.reshape(B, n_chunks, CHUNK, M_HEADS, M_HEAD_DIM).transpose(1, 0, 3, 2, 4)

    def gates(t):
        t = jnp.pad(t.astype(f32), ((0, 0), (0, pad), (0, 0)))
        return t.reshape(B, n_chunks, CHUNK, M_HEADS).transpose(1, 0, 3, 2)

    qc = heads(q)
    kc = heads(k) * (M_HEAD_DIM ** -0.5)
    vc = heads(v)
    logi = gates(i_pre)
    logf = jax.nn.log_sigmoid(gates(f_pre))
    causal = jnp.asarray(np.tril(np.ones((CHUNK, CHUNK), dtype=bool)))

    def step(carry, inp):
        C, n, m = carry
        qb, kb, vb, li, lf = inp
        b = jnp.cumsum(lf, axis=-1)
        Dm = jnp.where(causal, b[..., :, None] - b[..., None, :] + li[..., None, :], -jnp.inf)
        m_inter = b + m[..., None]
        m_t = jnp.maximum(m_inter, jnp.max(Dm, axis=-1))
        S = jnp.einsum('bhtd,bhsd->bhts', qb, kb) * jnp.exp(Dm - m_t[..., None])
        w_inter = jnp.exp(m_inter - m_t)
        num = jnp.einsum('bhts,bhsd->bhtd', S, vb) + w_inter[..., None] * jnp.einsum('bhvk,bhtk->bhtv', C, qb)
        den = jnp.sum(S, axis=-1) + w_inter * jnp.einsum('bhk,bhtk->bht', n, qb)
        h = num / jnp.maximum(jnp.abs(den), jnp.exp(-m_t))[..., None]
        b_end = b[..., -1]
        g = b_end[..., None] - b + li
        m_new = jnp.maximum(b_end + m, jnp.max(g, axis=-1))
        decay = jnp.exp(b_end + m - m_new)
        wg = jnp.exp(g - m_new[..., None])
        C = decay[..., None, None] * C + jnp.einsum('bhs,bhsv,bhsk->bhvk', wg, vb, kb)
        n = decay[..., None] * n + jnp.einsum('bhs,bhsk->bhk', wg, kb)
        return (C, n, m_new), h

    init = (jnp.zeros((B, M_HEADS, M_HEAD_DIM, M_HEAD_DIM), f32),
            jnp.zeros((B, M_HEADS, M_HEAD_DIM), f32),
            jnp.zeros((B, M_HEADS), f32))
    _, h = lax.scan(step, init, (qc, kc, vc, logi, logf))
    h = h.transpose(1, 0, 3, 2, 4).reshape(B, n_chunks * CHUNK, M_HEADS, M_HEAD_DIM)[:, :L]
    h = _rmsnorm(h, out_gain.reshape(M_HEADS, M_HEAD_DIM)).reshape(B, L, M_WIDTH)
    h = h * jax.nn.sigmoid(o_pre.astype(f32))
    return h.astype(q.dtype)

def _forgetting_attention(q, k, v, f_pre, g_q, g_k):
    B, L, _ = q.shape

    def heads(t):
        return t.reshape(B, L, F_HEADS, F_HEAD_DIM).transpose(0, 2, 1, 3)

    qh = _rmsnorm(heads(q), g_q)
    kh = _rmsnorm(heads(k), g_k)
    vh = heads(v)
    c = jnp.cumsum(jax.nn.log_sigmoid(f_pre.astype(jnp.float32)), axis=1).transpose(0, 2, 1)
    scale = F_HEAD_DIM ** -0.5
    outs = []
    for start in range(0, L, Q_BLOCK):
        end = min(start + Q_BLOCK, L)
        logits = jnp.einsum('bhtd,bhsd->bhts', qh[:, :, start:end], kh[:, :, :end]).astype(jnp.float32) * scale
        logits = logits + c[:, :, start:end, None] - c[:, :, None, :end]
        mask = np.arange(start, end)[:, None] >= np.arange(end)[None, :]
        logits = jnp.where(mask, logits, -jnp.inf)
        p = jax.nn.softmax(logits, axis=-1).astype(vh.dtype)
        outs.append(jnp.einsum('bhts,bhsd->bhtd', p, vh[:, :, :end]))
    out = jnp.concatenate(outs, axis=2)
    return out.transpose(0, 2, 1, 3).reshape(B, L, F_WIDTH)

def _peer(x, w_query, sub_keys, u_emb, v_emb):
    B, L, D = x.shape
    T = B * L
    Tp = -(-T // PEER_TOKEN_BLOCK) * PEER_TOKEN_BLOCK
    xt = jnp.pad(x.reshape(T, D), ((0, Tp - T), (0, 0))).reshape(-1, PEER_TOKEN_BLOCK, D)
    keys32 = sub_keys.astype(jnp.float32)

    def block(xb):
        tb = xb.shape[0]
        qh = (xb @ w_query).astype(jnp.float32).reshape(tb, PEER_HEADS, 2, PEER_HALF)
        scores = jnp.einsum('thpc,hpnc->thpn', qh, keys32)
        val, idx = lax.top_k(scores, PEER_TOPK)
        cand = (val[:, :, 0, :, None] + val[:, :, 1, None, :]).reshape(tb, PEER_HEADS, PEER_TOPK * PEER_TOPK)
        cand_id = (idx[:, :, 0, :, None] * N_KEYS + idx[:, :, 1, None, :]).reshape(tb, PEER_HEADS, PEER_TOPK * PEER_TOPK)
        top_s, pos = lax.top_k(cand, PEER_TOPK)
        ids = jnp.take_along_axis(cand_id, pos, axis=-1).reshape(tb, PEER_HEADS * PEER_TOPK)
        gate = jax.nn.softmax(top_s, axis=-1).reshape(tb, PEER_HEADS * PEER_TOPK)
        u = u_emb[ids]
        act = jax.nn.gelu(jnp.einsum('ted,td->te', u, xb).astype(jnp.float32), approximate=False)
        w = (gate * act).astype(xb.dtype)
        return jnp.einsum('te,ted->td', w, v_emb[ids])

    out = lax.map(block, xt)
    return out.reshape(Tp, D)[:T].reshape(B, L, D)

def first_inputs(seed: int = 0) -> dict:
    key = jax.random.key(seed)
    ks = jax.random.split(key, 20)
    f32 = jnp.float32
    nrm = lambda k, shape, s: jax.random.normal(k, shape, f32) * s
    fbias_m = jnp.broadcast_to(jnp.linspace(3.0, 6.0, M_HEADS, dtype=f32), (DEPTH, M_HEADS))
    fbias_f = jnp.broadcast_to(jnp.linspace(2.0, 6.0, F_HEADS, dtype=f32), (DEPTH, F_HEADS))
    return {
        "x": nrm(ks[0], (BATCH, SEQ, D_MODEL), 1.0),
        "meta_tokens": nrm(ks[1], (N_META, D_MODEL), 1.0),
        "norm_mix": 1.0 + nrm(ks[2], (DEPTH, D_MODEL), 0.02),
        "w_in": nrm(ks[3], (DEPTH, D_MODEL, PROJ_DIM), D_MODEL ** -0.5),
        "conv_qk": nrm(ks[4], (DEPTH, CONV_W, 2 * M_WIDTH), CONV_W ** -0.5),
        "b_igate": nrm(ks[5], (DEPTH, M_HEADS), 0.1),
        "b_fgate_m": fbias_m + nrm(ks[6], (DEPTH, M_HEADS), 0.1),
        "m_out_norm": 1.0 + nrm(ks[7], (DEPTH, M_WIDTH), 0.02),
        "b_fgate_f": fbias_f + nrm(ks[8], (DEPTH, F_HEADS), 0.1),
        "f_q_norm": 1.0 + nrm(ks[9], (DEPTH, F_HEAD_DIM), 0.02),
        "f_k_norm": 1.0 + nrm(ks[10], (DEPTH, F_HEAD_DIM), 0.02),
        "w_out": nrm(ks[11], (DEPTH, D_MIX, D_MODEL), D_MIX ** -0.5),
        "norm_ffn": 1.0 + nrm(ks[12], (DEPTH, D_MODEL), 0.02),
        "peer_query": nrm(ks[13], (DEPTH, D_MODEL, PEER_HEADS * PEER_QDIM), D_MODEL ** -0.5),
        "peer_sub_keys": nrm(ks[14], (DEPTH, PEER_HEADS, 2, N_KEYS, PEER_HALF), PEER_HALF ** -0.5),
        "peer_u": nrm(ks[15], (DEPTH, N_EXPERTS, D_MODEL), D_MODEL ** -0.5),
        "peer_v": nrm(ks[16], (DEPTH, N_EXPERTS, D_MODEL), 0.1),
    }

def first_block(x, meta_tokens, norm_mix, w_in, conv_qk, b_igate, b_fgate_m, m_out_norm,
              b_fgate_f, f_q_norm, f_k_norm, w_out, norm_ffn, peer_query, peer_sub_keys,
              peer_u, peer_v):
    B = x.shape[0]
    meta = jnp.broadcast_to(meta_tokens.astype(x.dtype)[None], (B, N_META, D_MODEL))
    h_res = jnp.concatenate([meta, x], axis=1)
    splits = _proj_splits()
    for layer in range(DEPTH):
        hn = _rmsnorm(h_res, norm_mix[layer])
        z = hn @ w_in[layer]
        mq, mk, mv, mo, mi, mf, fq, fk, fv, ff = jnp.split(z, splits, axis=-1)
        qk = jax.nn.silu(_causal_dwconv(jnp.concatenate([mq, mk], axis=-1), conv_qk[layer]))
        mq, mk = jnp.split(qk, 2, axis=-1)
        y_m = _mlstm(mq, mk, mv, mo, mi + b_igate[layer], mf + b_fgate_m[layer], m_out_norm[layer])
        y_f = _forgetting_attention(fq, fk, fv, ff + b_fgate_f[layer], f_q_norm[layer], f_k_norm[layer])
        h_res = h_res + jnp.concatenate([y_m, y_f], axis=-1) @ w_out[layer]
        if layer == DEPTH - 1:
            h_res = h_res[:, N_META:]
        h_res = h_res + _peer(_rmsnorm(h_res, norm_ffn[layer]), peer_query[layer],
                              peer_sub_keys[layer], peer_u[layer], peer_v[layer])
    return h_res


D_FF = 2816
FOURIER_GROUPS = 8
FOURIER_GROUP_DIM = 64
D_FOURIER = FOURIER_GROUPS * FOURIER_GROUP_DIM
D_SCONV = 512
SCONV_WIDTH = 3
DN_HEADS = 4
DN_HEAD_DIM = 128
D_DN = DN_HEADS * DN_HEAD_DIM
DN_CONV_WIDTH = 3
N_BRANCH = 3
PROJ_SIZES_2 = (D_FOURIER, 3 * D_SCONV, 3 * D_DN, D_DN, 2 * DN_HEADS, 2 * DN_HEADS, N_BRANCH * D_MODEL)
D_IN_PROJ = D_FOURIER + 3 * D_SCONV + 3 * D_DN + D_DN + 4 * DN_HEADS + N_BRANCH * D_MODEL


def rmsnorm(x, g):
    xf = x.astype(jnp.float32)
    y = xf * lax.rsqrt(jnp.mean(xf * xf, axis=-1, keepdims=True) + EPS)
    return (y * g.astype(jnp.float32)).astype(x.dtype)

def swiglu(x, wi, wo):
    a, b = jnp.split(x @ wi, 2, axis=-1)
    return (jax.nn.silu(a) * b) @ wo

def conv3_centred(x, w):
    xp = jnp.pad(x, ((0, 0), (1, 1), (0, 0)))
    return w[0] * xp[:, :-2] + w[1] * xp[:, 1:-1] + w[2] * xp[:, 2:]

def fourier_mix(u):
    B, L, _ = u.shape
    ug = u.astype(jnp.float32).reshape(B, L, FOURIER_GROUPS, FOURIER_GROUP_DIM)
    y = jnp.fft.fft2(ug, axes=(1, 3), norm="ortho").real
    return y.reshape(B, L, D_FOURIER).astype(u.dtype)

def short_conv_mix(u, w):
    b, c, h = jnp.split(u, 3, axis=-1)
    return b * conv3_centred(c * h, w)

def l2norm(x):
    return x * lax.rsqrt(jnp.sum(x * x, axis=-1, keepdims=True) + EPS)

def chunk_gated_delta(q, k, v, beta, g):
    B, H, N, C, DK = q.shape
    DV = v.shape[-1]
    lower = jnp.tril(jnp.ones((C, C), bool))
    strict = jnp.tril(jnp.ones((C, C), bool), -1)
    gc = jnp.cumsum(g, axis=-1)
    diff = gc[..., :, None] - gc[..., None, :]
    decay_mask = jnp.exp(jnp.where(lower, diff, -jnp.inf))
    k_beta = k * beta[..., None]
    v_beta = v * beta[..., None]
    m = jnp.where(strict, jnp.einsum('bhnck,bhnsk->bhncs', k_beta, k) * decay_mask, 0.0)
    eye = jnp.eye(C, dtype=q.dtype)
    t = lax.linalg.triangular_solve(eye + m, jnp.broadcast_to(eye, m.shape), left_side=True,
                                    lower=True, unit_diagonal=True)
    u = t @ v_beta
    w = t @ (k_beta * jnp.exp(gc)[..., None])
    attn = jnp.einsum('bhnck,bhnsk->bhncs', q, k) * decay_mask
    q_dec = q * jnp.exp(gc)[..., None]
    k_dec = k * jnp.exp(gc[..., -1:] - gc)[..., None]
    g_last = jnp.exp(gc[..., -1])

    def step(S, xs):
        attn_n, u_n, w_n, qd_n, kd_n, gl_n = xs
        v_new = u_n - w_n @ S
        o = qd_n @ S + attn_n @ v_new
        S = S * gl_n[..., None, None] + jnp.swapaxes(kd_n, -1, -2) @ v_new
        return S, o

    xs = tuple(jnp.moveaxis(a, 2, 0) for a in (attn, u, w, q_dec, k_dec, g_last))
    S0 = jnp.zeros((B, H, DK, DV), q.dtype)
    _, o = lax.scan(step, S0, xs)
    return jnp.moveaxis(o, 0, 2)

def deltanet_branch(qkv, z, beta_logit, alpha_logit, conv_w, A_log, dt_bias, norm_w):
    B, L, _ = qkv.shape
    f32 = jnp.float32
    qkv = jax.nn.silu(conv3_centred(qkv, conv_w)).astype(f32)
    q, k, v = jnp.split(qkv, 3, axis=-1)
    q = l2norm(q.reshape(B, L, DN_HEADS, DN_HEAD_DIM)) * (DN_HEAD_DIM ** -0.5)
    k = l2norm(k.reshape(B, L, DN_HEADS, DN_HEAD_DIM))
    v = v.reshape(B, L, DN_HEADS, DN_HEAD_DIM)
    beta = jax.nn.sigmoid(beta_logit.astype(f32)).reshape(B, L, 2, DN_HEADS)
    g = -jnp.exp(A_log.astype(f32)) * jax.nn.softplus(
        alpha_logit.astype(f32).reshape(B, L, 2, DN_HEADS) + dt_bias.astype(f32))
    pad = CHUNK - N_META
    padt = lambda a: jnp.pad(a, ((0, 0), (pad, 0)) + ((0, 0),) * (a.ndim - 2))
    q, k, v, beta, g = padt(q), padt(k), padt(v), padt(beta), padt(g)
    Lp = L + pad
    N = Lp // CHUNK

    def chunks4(a):
        return a.reshape(B, N, CHUNK, DN_HEADS, -1).transpose(0, 3, 1, 2, 4)

    def chunks3(a):
        return a.reshape(B, N, CHUNK, DN_HEADS).transpose(0, 3, 1, 2)

    def unchunk(o):
        return o.transpose(0, 2, 3, 1, 4).reshape(B, Lp, DN_HEADS, DN_HEAD_DIM)

    o_fwd = unchunk(chunk_gated_delta(chunks4(q), chunks4(k), chunks4(v),
                                      chunks3(beta[:, :, 0]), chunks3(g[:, :, 0])))
    fl = lambda a: jnp.flip(a, axis=1)
    o_bwd = fl(unchunk(chunk_gated_delta(chunks4(fl(q)), chunks4(fl(k)), chunks4(fl(v)),
                                         chunks3(fl(beta[:, :, 1])), chunks3(fl(g[:, :, 1])))))
    o = (o_fwd + o_bwd)[:, pad:]
    o = o * lax.rsqrt(jnp.mean(o * o, axis=-1, keepdims=True) + EPS) * norm_w.astype(f32)
    o = o * jax.nn.silu(z.astype(f32).reshape(B, L, DN_HEADS, DN_HEAD_DIM))
    return o.reshape(B, L, D_DN).astype(z.dtype)

def hybrid_mixer(h, w_in, sconv_w, dn_conv_w, dn_A_log, dn_dt_bias, dn_norm,
                 w_fourier, w_sconv_out, w_dn_out, w_out):
    B, L, D = h.shape
    proj = h @ w_in
    idx = [int(s) for s in np.cumsum(PROJ_SIZES_2)[:-1]]
    u_f, u_sc, u_qkv, z, b_logit, a_logit, gate_logit = jnp.split(proj, idx, axis=-1)
    y_f = fourier_mix(u_f) @ w_fourier
    y_sc = short_conv_mix(u_sc, sconv_w) @ w_sconv_out
    y_dn = deltanet_branch(u_qkv, z, b_logit, a_logit, dn_conv_w, dn_A_log, dn_dt_bias,
                           dn_norm) @ w_dn_out
    gates = jax.nn.sigmoid(gate_logit).reshape(B, L, N_BRANCH, D)
    merged = gates[:, :, 0] * y_f + gates[:, :, 1] * y_sc + gates[:, :, 2] * y_dn
    return merged @ w_out

def second_inputs(seed: int = 0) -> dict:
    key = jax.random.key(seed)
    ks = jax.random.split(key, 20)
    f32 = jnp.float32

    def dense(k, shape, fan_in):
        return jax.random.normal(k, shape, f32) * fan_in ** -0.5

    x = jax.random.normal(ks[0], (BATCH, SEQ, D_MODEL), f32)
    meta_tokens = jax.random.normal(ks[1], (N_META, D_MODEL), f32)
    norm_gains = 1.0 + 0.05 * jax.random.normal(ks[2], (DEPTH, 6, D_MODEL), f32)
    ffn1_wi = dense(ks[3], (DEPTH, D_MODEL, 2 * D_FF), D_MODEL)
    ffn1_wo = dense(ks[4], (DEPTH, D_FF, D_MODEL), D_FF)
    ffn2_wi = dense(ks[5], (DEPTH, D_MODEL, 2 * D_FF), D_MODEL)
    ffn2_wo = dense(ks[6], (DEPTH, D_FF, D_MODEL), D_FF)
    w_in = dense(ks[7], (DEPTH, D_MODEL, D_IN_PROJ), D_MODEL)
    sconv_w = dense(ks[8], (DEPTH, SCONV_WIDTH, D_SCONV), SCONV_WIDTH)
    dn_conv_w = dense(ks[9], (DEPTH, DN_CONV_WIDTH, 3 * D_DN), DN_CONV_WIDTH)
    dn_A_log = jnp.log(jax.random.uniform(ks[10], (DEPTH, 2, DN_HEADS), f32, 1.0, 16.0))
    dt = jnp.exp(jax.random.uniform(ks[11], (DEPTH, 2, DN_HEADS), f32,
                                    math.log(1e-3), math.log(1e-1)))
    dn_dt_bias = dt + jnp.log(-jnp.expm1(-dt))
    dn_norm = 1.0 + 0.05 * jax.random.normal(ks[12], (DEPTH, DN_HEAD_DIM), f32)
    w_fourier = dense(ks[13], (DEPTH, D_FOURIER, D_MODEL), D_FOURIER)
    w_sconv_out = dense(ks[14], (DEPTH, D_SCONV, D_MODEL), D_SCONV)
    w_dn_out = dense(ks[15], (DEPTH, D_DN, D_MODEL), D_DN)
    w_out = dense(ks[16], (DEPTH, D_MODEL, D_MODEL), D_MODEL)
    return {"x": x, "meta_tokens": meta_tokens, "norm_gains": norm_gains,
            "ffn1_wi": ffn1_wi, "ffn1_wo": ffn1_wo, "ffn2_wi": ffn2_wi, "ffn2_wo": ffn2_wo,
            "w_in": w_in, "sconv_w": sconv_w, "dn_conv_w": dn_conv_w, "dn_A_log": dn_A_log,
            "dn_dt_bias": dn_dt_bias, "dn_norm": dn_norm, "w_fourier": w_fourier,
            "w_sconv_out": w_sconv_out, "w_dn_out": w_dn_out, "w_out": w_out}

def second_block(x, meta_tokens, norm_gains, ffn1_wi, ffn1_wo, ffn2_wi, ffn2_wo, w_in, sconv_w,
              dn_conv_w, dn_A_log, dn_dt_bias, dn_norm, w_fourier, w_sconv_out, w_dn_out, w_out):
    B = x.shape[0]
    meta = jnp.broadcast_to(meta_tokens[None].astype(x.dtype), (B, N_META, D_MODEL))
    h = jnp.concatenate([meta, x], axis=1)
    for l in range(DEPTH):
        n = norm_gains[l]
        h = h + 0.5 * rmsnorm(swiglu(rmsnorm(h, n[0]), ffn1_wi[l], ffn1_wo[l]), n[1])
        h = h + rmsnorm(hybrid_mixer(rmsnorm(h, n[2]), w_in[l], sconv_w[l], dn_conv_w[l],
                                     dn_A_log[l], dn_dt_bias[l], dn_norm[l], w_fourier[l],
                                     w_sconv_out[l], w_dn_out[l], w_out[l]), n[3])
        h = h + 0.5 * rmsnorm(swiglu(rmsnorm(h, n[4]), ffn2_wi[l], ffn2_wo[l]), n[5])
    return h[:, N_META:]


def setup_inputs(seed=0):
    out = dict(first_inputs(seed))
    for name, value in second_inputs(seed + 1).items():
        if name != "x":
            out[name + "_2"] = value
    return out


def reference(
    x, meta_tokens, norm_mix, w_in, conv_qk, b_igate, b_fgate_m, m_out_norm, b_fgate_f,
    f_q_norm, f_k_norm, w_out, norm_ffn, peer_query, peer_sub_keys, peer_u, peer_v,
    meta_tokens_2, norm_gains_2, ffn1_wi_2, ffn1_wo_2, ffn2_wi_2, ffn2_wo_2, w_in_2, sconv_w_2,
    dn_conv_w_2, dn_A_log_2, dn_dt_bias_2, dn_norm_2, w_fourier_2, w_sconv_out_2, w_dn_out_2,
    w_out_2,
):
    x = first_block(
        x, meta_tokens, norm_mix, w_in, conv_qk, b_igate, b_fgate_m, m_out_norm, b_fgate_f,
        f_q_norm, f_k_norm, w_out, norm_ffn, peer_query, peer_sub_keys, peer_u, peer_v,
    )
    return second_block(
        x, meta_tokens_2, norm_gains_2, ffn1_wi_2, ffn1_wo_2, ffn2_wi_2, ffn2_wo_2, w_in_2,
        sconv_w_2, dn_conv_w_2, dn_A_log_2, dn_dt_bias_2, dn_norm_2, w_fourier_2, w_sconv_out_2,
        w_dn_out_2, w_out_2,
    )


_drawn_inputs = setup_inputs


def setup_inputs(seed=0):
    import zlib

    import numpy as np

    out = dict(_drawn_inputs(seed))
    spreads = {}
    factors = {'b_igate': 8.0,
     'm_out_norm': 4.64,
     'f_q_norm': 8.0,
     'f_k_norm': 8.0,
     'norm_ffn': 5.503,
     'dn_norm_2': 4.165}
    for name, (base, spread) in spreads.items():
        noise = np.random.default_rng([zlib.crc32(name.encode()), seed]).standard_normal(out[name].shape)
        drawn = base * np.exp(spread * noise) if base else spread * noise
        out[name] = __import__('jax').numpy.asarray(drawn.astype(out[name].dtype))
    for name, factor in factors.items():
        out[name] = (out[name] * factor).astype(out[name].dtype)
    return out
```

```python
from contextlib import ExitStack

import numpy as np

import concourse.bass as bass
from concourse import mybir

ALU = mybir.AluOpType
ACT = mybir.ActivationFunctionType
AX = mybir.AxisListType
F32 = mybir.dt.float32
U32 = mybir.dt.uint32

P = 128
D = 1024
META = 16
T = 512
L = T + META
HL = L // 2
DC = D // P
EPS = 1e-6
NEG = -1e30
TB = [(b * P, min(P, L - b * P)) for b in range((L + P - 1) // P)]
MH, FH, FD = 4, 8, 64
PH, NK, TOPK = 8, 128, 16
FF = 2816
FT = FF // P
DH = 4
CH = 88
NCH = L // CH
SUB = 16
SLOTS = 4
SLOT = 12 * P
WIDE = 512


def const_tables():
    i = np.arange(P)
    f = np.float32
    c = {}
    c["ident"] = np.eye(P)
    c["ones"] = np.ones((P, P))
    c["halves"] = (i[:, None] // FD == i[None, :] // FD)
    c["below"] = np.where(i[None, :] >= i[:, None], 0.0, NEG)
    c["above"] = np.where(i[None, :] <= i[:, None], 0.0, NEG)
    c["strict_f"] = np.where(i[None, :] < i[:, None], 0.0, -NEG)
    c["strict_b"] = np.where(i[None, :] > i[:, None], 0.0, -NEG)
    c["sub"] = (i[:, None] // SUB == i[None, :] // SUB)
    c["iota"] = np.tile(i[None, :], (P, 1))
    def sel(rows, cols, pairs, v):
        m = np.zeros((P, cols))
        for r, q in pairs:
            m[r, q] = v
        return m
    c["sel_i"] = sel(16, 4, [(h, h) for h in range(4)], 1)
    c["sel_nf"] = sel(16, 4, [(4 + h, h) for h in range(4)], -1)
    c["bc_nm"] = np.concatenate([sel(4, P, [(h, slice(None))], -1) for h in range(4)], 1)
    c["bc_nf"] = np.concatenate([sel(16, P, [(4 + h, slice(None))], -1) for h in range(4)], 1)
    c["bc_fox"] = np.concatenate([sel(16, P, [(8 + h, slice(None))], -float(FD) ** 0.5) for h in range(8)], 1)
    c["bc_g"] = np.concatenate([sel(16, P, [(8 + h, slice(None))], 1) for h in range(8)], 1)
    c["sel_gf"] = sel(16, 8, [(8 + h, h) for h in range(4)], 1)
    c["sel_gb"] = sel(16, 8, [(8 + h, h) for h in range(4, 8)], 1)
    c["sel_beta"] = sel(16, 8, [(h, h) for h in range(8)], 1)
    g = np.arange(64)
    w = 2 * np.pi * np.outer(g, g) / 64
    z = np.zeros((64, 64))
    c["dft_c"] = np.block([[np.cos(w), z], [z, np.cos(w)]]) / 8.0
    c["dft_s"] = np.block([[np.sin(w), z], [z, np.sin(w)]]) / 8.0
    return {k: np.ascontiguousarray(v, dtype=f) for k, v in c.items()}


CONST_COLS = {}
_at = 0
for _k, _n in [("ident", P), ("ones", P), ("halves", P), ("below", P), ("above", P), ("strict_f", P),
               ("strict_b", P), ("sub", P), ("iota", P), ("sel_i", 4), ("sel_nf", 4), ("bc_nm", 4 * P),
               ("bc_nf", 4 * P), ("bc_fox", 8 * P), ("bc_g", 8 * P), ("sel_gf", 8), ("sel_gb", 8),
               ("sel_beta", 8), ("dft_c", P), ("dft_s", P)]:
    CONST_COLS[_k] = (_at, _n)
    _at += _n
NCONST = _at

PARAM_COLS = {}
_at = 0
for _k, _n in [("norm_mix", 8), ("norm_ffn", 8), ("gains2", 48), ("conv1", 32), ("m_out", 4), ("fq", 2),
               ("fk", 1), ("bias1", 1), ("sconv", 12), ("dnconv", 36), ("alog", 1), ("dt", 1), ("dn", 1)]:
    PARAM_COLS[_k] = (_at, _n)
    _at += _n
NPARAM = _at


class Steps:

    def __init__(self, sem, names, looped=False):
        self.sem, self.names, self.looped = sem, list(names), looped
        self.index = {n: i for i, n in enumerate(self.names)}
        assert len(self.index) == len(self.names)

    def at(self, eng, name, turn=0):
        v = turn * len(self.names) + (self.index[name] + (1 if self.looped else 0))
        if not isinstance(v, int) or v > 0:
            eng.wait_ge(self.sem, v)

    def done(self, ins):
        ins.then_inc(self.sem, 1)


class Env:
    pass


def weights(e, name):
    return e.w[name]


def stream(e, sp, name, nxt):
    w, n = e.w[name], e.w[name].shape[0]
    cols = w.shape[2]
    g0 = e.base[name]
    if n > SLOTS:
        with sp.Fori(0, n // SLOTS - 1) as it:
            for k in range(SLOTS):
                sp.wait_ge(e.tiles_used, it * SLOTS + (g0 + k + 1))
                sp.dma_start(e.ring[:, k, 0:cols], w[it * SLOTS + (SLOTS + k)]).then_inc(e.slot_full[k], 16)
    if nxt:
        prefetch(e, sp, nxt, g0 + n)


def prefetch(e, sp, name, used):
    w = e.w[name]
    cols = w.shape[2]
    for k in range(SLOTS):
        if used:
            sp.wait_ge(e.tiles_used, used - SLOTS + k + 1)
        sp.dma_start(e.ring[:, k, 0:cols], w[k]).then_inc(e.slot_full[k], 16)


def slot_wait(e, pe, name, it, k):
    pe.wait_ge(e.slot_full[k], it * 16 + 16 * (e.base[name] // SLOTS + 1))


def tile_matmuls(nc, e, k, blocks, rhs, banks, off=0, t0=0, n=HL):
    for hf in range(2):
        for c in range(blocks):
            mm = nc.tensor.matmul(e.ps[:, banks + hf, 0:n], e.ring[:, k, (off + c) * P:(off + c + 1) * P],
                                  rhs(c, hf), start=(c == 0), stop=(c == blocks - 1))
    return mm


def halves(ap):
    return ap.rearrange("p (h t) -> p h t", h=2)


def half(ap, hf):
    return ap[:, hf * HL:(hf + 1) * HL]


def phase_linear(nc, e, name, nxt, src, n, evac):
    ready, taken = e.sem(f"{name}_ready"), e.sem(f"{name}_taken")
    loops = n // SLOTS
    with nc.Block() as block:
        @block.sync
        def _(sp):
            stream(e, sp, name, nxt)

        @block.tensor
        def _(pe):
            def body(it, first):
                for k in range(SLOTS):
                    slot_wait(e, pe, name, it, k)
                    if not first:
                        pe.wait_ge(taken, it * SLOTS + (k + 1 - SLOTS))
                    tile_matmuls(nc, e, k, DC, lambda c, hf: half(src[:, c], hf), 2 * k).then_inc(e.tiles_used, 1)
            body(0, True)
            if loops > 1:
                with pe.Fori(1, loops) as it:
                    body(it, False)

        @block.scalar
        def _(act):
            if evac[0] != "act":
                return
            with act.Fori(0, loops) as it:
                for k in range(SLOTS):
                    act.wait_ge(e.tiles_used, it * SLOTS + (e.base[name] + k + 1))
                    evac[1](it, k, e.ps[:, 2 * k:2 * k + 2, 0:HL]).then_inc(taken, 1)

        @block.vector
        def _(dve):
            if evac[0] != "dve":
                return
            with dve.Fori(0, loops) as it:
                for k in range(SLOTS):
                    dve.wait_ge(e.tiles_used, it * SLOTS + (e.base[name] + k + 1))
                    evac[1](it, k, e.ps[:, 2 * k:2 * k + 2, 0:HL]).then_inc(taken, 1)


def phase_norm(nc, e, tag, src, gain, dst, tail=None):
    sq_done, sum_done = e.sem(f"{tag}_sq"), e.sem(f"{tag}_sum")
    st = Steps(e.sem(f"{tag}_rstd"), ["sqrt", "recip", "apply"])
    add = e.sem(f"{tag}_add")
    with nc.Block() as block:
        @block.scalar
        def _(act):
            for c in range(DC):
                if c % 2 == 0:
                    if c >= 4:
                        act.wait_ge(sum_done, c - 3)
                    nc.scalar.activation(e.sq[:, c % 4], src[:, c], ACT.Square).then_inc(sq_done, 1)
            act.wait_ge(sum_done, DC)
            nc.scalar.activation(halves(e.r0), e.ps[:, 0:2, 0:HL], ACT.Sqrt, bias=e.eps[:, 0:1],
                                 scale=1.0 / D).then_inc(st.sem, 1)

        sq_odd = e.sem(f"{tag}_sqo")

        @block.tensor
        def _(pe):
            for c in range(DC):
                pe.wait_ge(sq_done if c % 2 == 0 else sq_odd, c // 2 + 1)
                for hf in range(2):
                    mm = nc.tensor.matmul(e.ps[:, hf, 0:HL], e.c["ones"], half(e.sq[:, c % 4], hf),
                                          start=(c == 0), stop=(c == DC - 1), skip_group_check=True)
                mm.then_inc(sum_done, 1)

        @block.vector
        def _(dve):
            for c in range(1, DC, 2):
                if c >= 4:
                    dve.wait_ge(sum_done, c - 3)
                nc.vector.tensor_tensor(e.sq[:, c % 4], src[:, c], src[:, c], ALU.mult).then_inc(sq_odd, 1)
            st.at(dve, "recip")
            nc.vector.reciprocal(e.r1, e.r0).then_inc(st.sem, 1)
            st.at(dve, "apply")
            for c in range(DC):
                nc.vector.scalar_tensor_tensor(out=dst[:, c], in0=src[:, c], scalar=gain[:, c:c + 1], in1=e.r1,
                                               op0=ALU.mult, op1=ALU.mult).then_inc(st.sem, 1)
                if tail is not None:
                    dve.wait_ge(st.sem, 3 + c)
                    nc.vector.scalar_tensor_tensor(out=e.h[:, c], in0=dst[:, c], scalar=tail, in1=e.h[:, c],
                                                   op0=ALU.mult, op1=ALU.add).then_inc(add, 1)


def phase_head_norm(nc, e, tag, tiles, mat, scale, gains, outs=None, mul=None):
    names = ["sq", "sum", "sqrt", "recip", "apply"] + (["mul"] if mul is not None else [])
    st = [Steps(e.sem(f"{tag}{b}"), names) for b in range(2)]
    n = len(tiles)
    rr = [e.r0, e.r1]
    with nc.Block() as block:
        @block.scalar
        def _(act):
            for i in range(0, n, 2):
                for b in range(2):
                    st[b].at(act, "sq", i // 2)
                    nc.scalar.activation(e.sq[:, b], tiles[i + b], ACT.Square).then_inc(st[b].sem, 1)
                for b in range(2):
                    st[b].at(act, "sqrt", i // 2)
                    nc.scalar.activation(halves(rr[b]), e.ps[:, 2 * b:2 * b + 2, 0:HL], ACT.Sqrt,
                                         bias=e.eps[:, 0:1], scale=scale).then_inc(st[b].sem, 1)

        @block.tensor
        def _(pe):
            for i in range(0, n, 2):
                for b in range(2):
                    st[b].at(pe, "sum", i // 2)
                    for hf in range(2):
                        mm = nc.tensor.matmul(e.ps[:, 2 * b + hf, 0:HL], mat, half(e.sq[:, b], hf))
                    mm.then_inc(st[b].sem, 1)

        @block.vector
        def _(dve):
            for i in range(0, n, 2):
                for b in range(2):
                    st[b].at(dve, "recip", i // 2)
                    nc.vector.reciprocal(e.sq[:, 2 + b], rr[b]).then_inc(st[b].sem, 1)
                    st[b].at(dve, "apply", i // 2)
                    x = tiles[i + b]
                    for o, g in zip(outs[i + b] if outs else [x], gains[i + b]):
                        ap = nc.vector.scalar_tensor_tensor(out=o, in0=x, scalar=g, in1=e.sq[:, 2 + b],
                                                            op0=ALU.mult, op1=ALU.mult)
                    ap.then_inc(st[b].sem, 1)
                    if mul is not None:
                        st[b].at(dve, "mul", i // 2)
                        nc.vector.tensor_tensor(x, x, mul[i + b], ALU.mult).then_inc(st[b].sem, 1)



def phase_conv_silu(nc, e, tag, tiles, taps):
    k = len(taps[0])
    st = [Steps(e.sem(f"{tag}{b}"), [f"tap{j}" for j in range(k)] + ["silu"]) for b in range(2)]
    with nc.Block() as block:
        @block.vector
        def _(dve):
            for i in range(len(tiles)):
                x, out, s = tiles[i], e.sq[:, i % 2], st[i % 2]
                for j, (d, w) in enumerate(taps[i]):
                    s.at(dve, f"tap{j}", i // 2)
                    if d == 0:
                        nc.vector.tensor_scalar(out, x, w, None, ALU.mult).then_inc(s.sem, 1)
                    else:
                        o = out[:, -d:L] if d < 0 else out[:, 0:L - d]
                        xi = x[:, 0:L + d] if d < 0 else x[:, d:L]
                        nc.vector.scalar_tensor_tensor(out=o, in0=xi, scalar=w, in1=o, op0=ALU.mult,
                                                       op1=ALU.add).then_inc(s.sem, 1)

        @block.scalar
        def _(act):
            for i in range(len(tiles)):
                s = st[i % 2]
                s.at(act, "silu", i // 2)
                nc.scalar.activation(tiles[i], e.sq[:, i % 2], ACT.Silu).then_inc(s.sem, 1)


def phase_values(nc, e, nxt, src, vt):
    name = "w_v"
    out, taken = e.sem("v_out"), e.sem("v_taken")
    nb = len(TB)
    with nc.Block() as block:
        @block.sync
        def _(sp):
            stream(e, sp, name, nxt)

        @block.tensor
        def _(pe):
            for it in range(2):
                for k in range(SLOTS):
                    slot_wait(e, pe, name, it, k)
                for b, (t0, rows) in enumerate(TB):
                    if it:
                        pe.wait_ge(taken, b + 1)
                    for c in range(DC):
                        mm = nc.tensor.matmul(e.ps[0:rows, b, :], src[:, c, t0:t0 + rows],
                                              e.ring[:, :, c * P:(c + 1) * P], start=(c == 0), stop=(c == DC - 1))
                    if b < nb - 1:
                        mm.then_inc(out, 1)
                mm.then_inc(e.tiles_used, SLOTS)

        @block.scalar
        def _(act):
            for it in range(2):
                for b, (t0, rows) in enumerate(TB):
                    if b < nb - 1:
                        act.wait_ge(out, it * (nb - 1) + b + 1)
                    else:
                        act.wait_ge(e.tiles_used, e.base[name] + SLOTS * (it + 1))
                    nc.scalar.activation(vt[0:rows, b, it * WIDE:(it + 1) * WIDE], e.ps[0:rows, b, :],
                                         ACT.Copy).then_inc(taken, 1)


def phase_gates1(nc, e, src, g):
    st = Steps(e.sem("g1"), ["z", "bias", "abs", "exp", "ln", "min", "lf", "cum", "a", "runmax", "at", "evac"])
    with nc.Block() as block:
        @block.tensor
        def _(pe):
            for hf in range(2):
                for c in range(DC):
                    mm = nc.tensor.matmul(e.ps[0:16, hf, 0:HL], e.wg1[:, c], half(src[:, c], hf),
                                          start=(c == 0), stop=(c == DC - 1))
            mm.then_inc(st.sem, 1)
            st.at(pe, "a")
            for hf in range(2):
                nc.tensor.matmul(e.ps[0:4, 2 + hf, 0:HL], e.c["sel_i"][0:16], half(g.raw, hf), start=True, stop=False)
                mm = nc.tensor.matmul(e.ps[0:4, 2 + hf, 0:HL], e.c["sel_nf"][0:16], half(g.cum, hf),
                                      start=False, stop=True)
            mm.then_inc(st.sem, 1)
            st.at(pe, "at")
            for b, (t0, rows) in enumerate(TB):
                nc.tensor.matmul(e.ps[0:rows, 4, 4 * b:4 * b + 4], g.raw[:, t0:t0 + rows], e.c["sel_i"][0:16],
                                 start=True, stop=False)
                mm = nc.tensor.matmul(e.ps[0:rows, 4, 4 * b:4 * b + 4], g.cum[:, t0:t0 + rows],
                                      e.c["sel_nf"][0:16], start=False, stop=True)
            mm.then_inc(st.sem, 1)

        @block.scalar
        def _(act):
            st.at(act, "bias")
            nc.scalar.activation(halves(g.raw), e.ps[0:16, 0:2, 0:HL], ACT.Identity,
                                 bias=e.p["bias1"][0:16]).then_inc(st.sem, 1)
            st.at(act, "abs")
            nc.scalar.activation(g.t1, g.raw, ACT.Abs).then_inc(st.sem, 1)
            st.at(act, "exp")
            nc.scalar.activation(g.t2, g.t1, ACT.Exp, scale=-1.0).then_inc(st.sem, 1)
            st.at(act, "ln")
            nc.scalar.activation(g.t1, g.t2, ACT.Ln, bias=e.one[0:16]).then_inc(st.sem, 1)

        @block.vector
        def _(dve):
            st.at(dve, "min")
            nc.vector.tensor_scalar(g.t2, g.raw, 0.0, None, ALU.min).then_inc(st.sem, 1)
            st.at(dve, "lf")
            nc.vector.tensor_tensor(g.t2, g.t2, g.t1, ALU.subtract).then_inc(st.sem, 1)
            st.at(dve, "cum")
            nc.vector.tensor_tensor_scan(g.cum, e.ones_row[0:16], g.t2, 0.0, ALU.mult, ALU.add).then_inc(st.sem, 1)
            st.at(dve, "runmax")
            nc.vector.tensor_tensor_scan(g.rmax[:, 0:HL], e.ps[0:4, 2, 0:HL], e.zero_row[0:4, 0:HL], 0.0, ALU.max,
                                         ALU.add).then_inc(e.sem("g1_firsthalf"), 1)
            dve.wait_ge(e.sems["g1_firsthalf"], 1)
            nc.vector.tensor_tensor_scan(g.rmax[:, HL:L], e.ps[0:4, 3, 0:HL], e.zero_row[0:4, 0:HL],
                                         g.rmax[:, HL - 1:HL], ALU.max, ALU.add).then_inc(st.sem, 1)
            st.at(dve, "evac")
            nc.vector.tensor_copy(g.acol[:, 0:4], e.ps[:, 4, 0:16].rearrange("p (b h) -> p b h", h=4))
            nc.vector.tensor_copy(g.acol[0:16, 4], e.ps[0:16, 4, 16:20]).then_inc(st.sem, 1)


def pieces(t0):
    return [(a, b) for a, b in ((t0, WIDE), (WIDE, L)) if a < b]


def phase_mlstm(nc, e, g, q, k, vt, y):
    names = ["nm", "diag"]
    for b in range(len(TB)):
        names += [f"scores{b}", f"exp{b}", f"weigh{b}", f"sum{b}"]
    names += ["mrow", "guard", "abs", "max", "recip", "out"]
    st = Steps(e.sem("ml"), names)
    nm, sc, num, den = 0, 1024, 2048, 3072
    psf, c = e.psf, e.c
    with nc.Block() as block:
        @block.tensor
        def _(pe):
            for h in range(MH):
                st.at(pe, "nm", h)
                for a, b in pieces(0):
                    mm = nc.tensor.matmul(psf[:, nm + a:nm + b], c["bc_nm"][0:4, h * P:(h + 1) * P], g.rmax[:, a:b])
                mm.then_inc(st.sem, 1)
                for sb, (t0, rows) in enumerate(TB):
                    st.at(pe, f"scores{sb}", h)
                    for a, b in pieces(t0):
                        mm = nc.tensor.matmul(psf[0:rows, sc + a:sc + b], k[:, h, t0:t0 + rows], q[:, h, a:b])
                    mm.then_inc(st.sem, 1)
                    st.at(pe, f"sum{sb}", h)
                    last = sb == len(TB) - 1
                    for a, b in pieces(t0):
                        end = last if b == L else sb == len(TB) - 2
                        nc.tensor.matmul(psf[:, num + a:num + b], vt[0:rows, sb, h * P:(h + 1) * P],
                                         e.pt[0:rows, a:b], start=(sb == 0), stop=end)
                        mm = nc.tensor.matmul(psf[:, den + a:den + b], c["ones"][0:rows], e.pt[0:rows, a:b],
                                              start=(sb == 0), stop=end)
                    mm.then_inc(st.sem, 1)
                st.at(pe, "mrow", h)
                for a, b in pieces(0):
                    nc.tensor.matmul(psf[:, sc + a:sc + b], c["bc_nm"][0:4, h * P:(h + 1) * P], g.rmax[:, a:b],
                                     start=True, stop=False)
                    mm = nc.tensor.matmul(psf[:, sc + a:sc + b], c["bc_nf"][0:16, h * P:(h + 1) * P], g.cum[:, a:b],
                                          start=False, stop=True)
                mm.then_inc(st.sem, 1)

        @block.scalar
        def _(act):
            for h in range(MH):
                for sb, (t0, rows) in enumerate(TB):
                    st.at(act, f"exp{sb}", h)
                    ex = nc.scalar.activation(e.et[0:rows, t0:t0 + rows], e.dg[0:rows, t0:t0 + rows], ACT.Exp,
                                              bias=g.acol[0:rows, sb, h:h + 1])
                    if t0 + rows < L:
                        ex = nc.scalar.activation(e.et[0:rows, t0 + rows:L], psf[0:rows, nm + t0 + rows:nm + L],
                                                  ACT.Exp, bias=g.acol[0:rows, sb, h:h + 1])
                    ex.then_inc(st.sem, 1)
                st.at(act, "guard", h)
                nc.scalar.activation(e.r0, psf[:, sc:sc + L], ACT.Exp).then_inc(st.sem, 1)
                st.at(act, "abs", h)
                nc.scalar.activation(e.r1, psf[:, den:den + L], ACT.Abs).then_inc(st.sem, 1)

        @block.vector
        def _(dve):
            for h in range(MH):
                st.at(dve, "diag", h)
                for t0, rows in TB:
                    dg = nc.vector.tensor_tensor(e.dg[0:rows, t0:t0 + rows], psf[0:rows, nm + t0:nm + t0 + rows],
                                                 c["below"][0:rows, 0:rows], ALU.add)
                dg.then_inc(st.sem, 1)
                for sb, (t0, rows) in enumerate(TB):
                    st.at(dve, f"weigh{sb}", h)
                    nc.vector.scalar_tensor_tensor(out=e.pt[0:rows, t0:L], in0=psf[0:rows, sc + t0:sc + L],
                                                   scalar=float(P) ** -0.5, in1=e.et[0:rows, t0:L], op0=ALU.mult,
                                                   op1=ALU.mult).then_inc(st.sem, 1)
                st.at(dve, "max", h)
                nc.vector.tensor_tensor(e.r0, e.r0, e.r1, ALU.max).then_inc(st.sem, 1)
                st.at(dve, "recip", h)
                nc.vector.reciprocal(e.r1, e.r0).then_inc(st.sem, 1)
                st.at(dve, "out", h)
                nc.vector.tensor_tensor(y[:, h], psf[:, num:num + L], e.r1, ALU.mult).then_inc(st.sem, 1)


def phase_fox(nc, e, g, qz, k, vt, yt, yT):
    st = [Steps(e.sem(f"fox{b}"), ["scores", "max", "neg", "exp", "recip", "turn", "evac", "mix", "out"])
          for b in range(2)]
    items = [(h, b) for b in range(len(TB)) for h in range(FH)]
    scale = float(FD) ** -0.5
    psf, c = e.psf, e.c
    tr = Steps(e.sem("fox_turn"), ["turn", "evac"])
    with nc.Block() as block:
        @block.tensor
        def _(pe):
            def scores(n):
                (h, b), s, base = items[n], st[n % 2], (n % 2) * 2048
                t0, rows = TB[b]
                s.at(pe, "scores", n // 2)
                for a, z in [(x, y) for x, y in ((0, WIDE), (WIDE, L)) if x < t0 + rows]:
                    z = min(z, t0 + rows)
                    o = psf[0:rows, base + a:base + z]
                    diag = z == t0 + rows
                    nc.tensor.matmul(o, qz[:, h, t0:t0 + rows], k[:, h // 2, a:z], start=True, stop=False)
                    mm = nc.tensor.matmul(o, c["bc_fox"][0:16, h * P:h * P + rows], g.cum[:, a:z], start=False,
                                          stop=not diag)
                    if diag:
                        mm = nc.tensor.matmul(psf[0:rows, base + t0:base + t0 + rows], c["ident"][0:rows, 0:rows],
                                              c["above"][0:rows, 0:rows], start=False, stop=True)
                mm.then_inc(s.sem, 1)

            def turn(n):
                (h, b), s, base = items[n], st[n % 2], (n % 2) * 2048 + 1024
                s.at(pe, "turn", n // 2)
                rows = TB[b][1]
                for j in range(b + 1):
                    cols = TB[j][1]
                    mm = nc.tensor.transpose(psf[0:cols, base + j * P:base + j * P + rows],
                                             e.fp[0:rows, n % 2, j * P:j * P + cols], c["ident"][0:rows, 0:rows])
                mm.then_inc(s.sem, 1)

            def mix(n):
                (h, b), s, base = items[n], st[n % 2], (n % 2) * 2048
                s.at(pe, "mix", n // 2)
                rows = TB[b][1]
                for j in range(b + 1):
                    cols = TB[j][1]
                    mm = nc.tensor.matmul(psf[0:rows, base:base + FD], e.fpT[0:cols, n % 2, j, 0:rows],
                                          vt[0:cols, j, WIDE + h * FD:WIDE + (h + 1) * FD],
                                          start=(j == 0), stop=(j == b))
                mm.then_inc(s.sem, 1)

            for n in range(0, len(items), 2):
                for f in (scores, turn, mix):
                    f(n)
                    f(n + 1)
            for i in range(4):
                if i == 0:
                    for s in st:
                        pe.wait_ge(s.sem, len(s.names) * (len(items) // 2))
                tr.at(pe, "turn", i)
                for b, (t0, rows) in enumerate(TB):
                    mm = nc.tensor.transpose(psf[:, t0:t0 + rows], yt[0:rows, b, i * P:(i + 1) * P],
                                             c["ident"][0:rows, 0:rows])
                mm.then_inc(tr.sem, 1)

        @block.scalar
        def _(act):
            for n0 in range(0, len(items), 2):
                for n in (n0, n0 + 1):
                    (h, b), s, base = items[n], st[n % 2], (n % 2) * 2048
                    t0, rows = TB[b]
                    s.at(act, "exp", n // 2)
                    nc.scalar.activation(e.fp[0:rows, n % 2, 0:t0 + rows], psf[0:rows, base:base + t0 + rows], ACT.Exp,
                                         bias=e.fmx[0:rows, n % 2, 1:2], scale=scale,
                                         accum_out=e.fmx[0:rows, n % 2, 2:3]).then_inc(s.sem, 1)
                for n in (n0, n0 + 1):
                    (h, b), s, base = items[n], st[n % 2], (n % 2) * 2048 + 1024
                    t0, rows = TB[b]
                    s.at(act, "evac", n // 2)
                    if b:
                        cp = nc.scalar.activation(e.fpT[:, n % 2, 0:b, 0:rows],
                                                  psf[:, base:base + b * P].rearrange("p (j t) -> p j t", t=P)[:, :, 0:rows],
                                                  ACT.Copy)
                    cp = nc.scalar.activation(e.fpT[0:rows, n % 2, b, 0:rows], psf[0:rows, base + t0:base + t0 + rows],
                                              ACT.Copy)
                    cp.then_inc(s.sem, 1)
            for i in range(4):
                tr.at(act, "evac", i)
                nc.scalar.activation(yT[:, i], psf[:, 0:L], ACT.Copy).then_inc(tr.sem, 1)

        @block.vector
        def _(dve):
            for n0 in range(0, len(items), 2):
                for n in (n0, n0 + 1):
                    (h, b), s, base = items[n], st[n % 2], (n % 2) * 2048
                    t0, rows = TB[b]
                    m = e.fmx[0:rows, n % 2]
                    s.at(dve, "max", n // 2)
                    nc.vector.tensor_reduce(m[:, 0:1], psf[0:rows, base:base + t0 + rows], AX.X, ALU.max).then_inc(s.sem, 1)
                    s.at(dve, "neg", n // 2)
                    nc.vector.tensor_scalar(m[:, 1:2], m[:, 0:1], -scale, None, ALU.mult).then_inc(s.sem, 1)
                for n in (n0, n0 + 1):
                    (h, b), s = items[n], st[n % 2]
                    rows = TB[b][1]
                    m = e.fmx[0:rows, n % 2]
                    s.at(dve, "recip", n // 2)
                    nc.vector.reciprocal(m[:, 3:4], m[:, 2:3]).then_inc(s.sem, 1)
                for n in (n0, n0 + 1):
                    (h, b), s, base = items[n], st[n % 2], (n % 2) * 2048
                    rows = TB[b][1]
                    s.at(dve, "out", n // 2)
                    nc.vector.tensor_scalar(yt[0:rows, b, h * FD:(h + 1) * FD], psf[0:rows, base:base + FD],
                                            e.fmx[0:rows, n % 2, 3:4], None, ALU.mult).then_inc(s.sem, 1)


def phase_topk(nc, e, qT, keys, k):
    one = ["max1", "idx1", "drop", "max2", "idx2"]
    names = (["scores", "evac"] + one + ["cand"] + ["c" + n for n in one] + ["sub", "exp", "split", "cvt", "total",
             "recip", "gate", "eq0", "mul0", "red0", "eq1", "mul1", "red1", "turn", "tevac"])
    nb = T // P
    st = [Steps(e.sem(f"topk{b}"), names) for b in range(2)]
    psf, c = e.psf, e.c
    with nc.Block() as block:
        @block.tensor
        def _(pe):
            for n0 in range(0, nb, 2):
                for n in (n0, n0 + 1):
                    s, base = st[n % 2], (n % 2) * 2048
                    s.at(pe, "scores", n // 2)
                    for j in range(2 * PH):
                        mm = nc.tensor.matmul(psf[:, base + j * NK:base + (j + 1) * NK], qT[:, j, n * P:(n + 1) * P],
                                              keys[:, j])
                    mm.then_inc(s.sem, 1)
                for n in (n0, n0 + 1):
                    s, base = st[n % 2], (n % 2) * 2048
                    s.at(pe, "turn", n // 2)
                    for j, x in enumerate((k[n % 2].row, k[n % 2].col, k[n % 2].gate)):
                        mm = nc.tensor.transpose(psf[:, base + j * P:base + (j + 1) * P],
                                                 x.rearrange("p h r -> p (h r)"), c["ident"])
                    mm.then_inc(s.sem, 1)

        @block.scalar
        def _(act):
            for n0 in range(0, nb, 2):
                for n in (n0, n0 + 1):
                    s, b = st[n % 2], k[n % 2]
                    s.at(act, "evac", n // 2)
                    nc.scalar.activation(b.sc.rearrange("p j n -> p (j n)"), psf[:, (n % 2) * 2048:(n % 2 + 1) * 2048],
                                         ACT.Copy).then_inc(s.sem, 1)
                for n in (n0, n0 + 1):
                    s, b = st[n % 2], k[n % 2]
                    s.at(act, "exp", n // 2)
                    nc.scalar.activation(b.gate, b.gate, ACT.Exp).then_inc(s.sem, 1)
                for n in (n0, n0 + 1):
                    s, b = st[n % 2], k[n % 2]
                    s.at(act, "tevac", n // 2)
                    for j, x in enumerate((e.rowT, e.colT, e.gateT)):
                        base = (n % 2) * 2048 + j * P
                        cp = nc.scalar.activation(x[:, n * P:(n + 1) * P], psf[:, base:base + P], ACT.Copy)
                    cp.then_inc(s.sem, 1)

        @block.vector
        def _(dve):
            def top16(s, turn, pre, n, x, val, idx):
                for name, f in (
                    (one[0], lambda j: nc.vector.max(val[:, j, 0:8], x[:, j])),
                    (one[1], lambda j: nc.vector.max_index(idx[:, j, 0:8], val[:, j, 0:8], x[:, j])),
                    (one[2], lambda j: nc.vector.match_replace(x[:, j], val[:, j, 0:8], x[:, j], -3.0e38)),
                    (one[3], lambda j: nc.vector.max(val[:, j, 8:16], x[:, j])),
                    (one[4], lambda j: nc.vector.max_index(idx[:, j, 8:16], val[:, j, 8:16], x[:, j])),
                ):
                    s.at(dve, pre + name, turn)
                    for j in range(n):
                        ins = f(j)
                    ins.then_inc(s.sem, 1)

            def bc_last(x):
                return x.unsqueeze(3).broadcast_to([P, PH, TOPK, TOPK])

            def bc_mid(x):
                return x.unsqueeze(2).broadcast_to([P, PH, TOPK, TOPK])

            for n in range(nb):
                s, b, u = st[n % 2], k[n % 2], n // 2
                V = nc.vector
                top16(s, u, "", 2 * PH, b.sc, b.val, b.idx)
                s.at(dve, "cand", u)
                val = b.val.rearrange("p (h two) r -> p h two r", two=2)
                idx = b.idxf.rearrange("p (h two) r -> p h two r", two=2)
                cand = b.sc.rearrange("p j n -> p (j n)").rearrange("p (h a b) -> p h a b", h=PH, a=TOPK)
                V.tensor_tensor(cand, bc_last(val[:, :, 0]), bc_mid(val[:, :, 1]), ALU.add).then_inc(s.sem, 1)
                top16(s, u, "c", PH, b.sc.rearrange("p j n -> p (j n)").rearrange("p (h x) -> p h x", h=PH), b.top, b.pos)
                s.at(dve, "sub", u)
                V.tensor_tensor(b.gate, b.top, b.top[:, :, 0:1].broadcast_to([P, PH, TOPK]),
                                ALU.subtract).then_inc(s.sem, 1)
                s.at(dve, "split", u)
                V.tensor_scalar(b.hi, b.pos, 4, None, ALU.logical_shift_right)
                V.tensor_scalar(b.lo, b.pos, 15, None, ALU.bitwise_and).then_inc(s.sem, 1)
                s.at(dve, "cvt", u)
                V.tensor_copy(b.hif, b.hi)
                V.tensor_copy(b.lof, b.lo)
                V.tensor_copy(b.idxf, b.idx).then_inc(s.sem, 1)
                s.at(dve, "total", u)
                V.tensor_reduce(b.tot, b.gate, AX.X, ALU.add).then_inc(s.sem, 1)
                s.at(dve, "recip", u)
                V.reciprocal(b.rec, b.tot).then_inc(s.sem, 1)
                s.at(dve, "gate", u)
                V.tensor_tensor(b.gate, b.gate, b.rec.unsqueeze(2).broadcast_to([P, PH, TOPK]),
                                ALU.mult).then_inc(s.sem, 1)
                rank = c["iota"][:, 0:TOPK].unsqueeze(1).unsqueeze(1).broadcast_to([P, PH, TOPK, TOPK])
                for j, (pos, out) in enumerate(((b.hif, b.row), (b.lof, b.col))):
                    s.at(dve, f"eq{j}", u)
                    V.tensor_tensor(cand, bc_last(pos), rank, ALU.is_equal).then_inc(s.sem, 1)
                    s.at(dve, f"mul{j}", u)
                    V.tensor_tensor(cand, cand, bc_mid(idx[:, :, j]), ALU.mult).then_inc(s.sem, 1)
                    s.at(dve, f"red{j}", u)
                    V.tensor_reduce(out, cand, AX.X, ALU.add).then_inc(s.sem, 1)


GT = 4
GB = 64
GN = GB // GT


def phase_gate_table(nc, e, b):
    hot, outer, stored, saved = e.sem("hot"), e.sem("outer"), e.sem("stored"), [e.sem(f"saved{x}") for x in range(2)]
    nblk = T // GB
    with nc.Block() as block:
        @block.vector
        def _(dve):
            for blk in range(nblk):
                with dve.Fori(0, GN // 4) as it:
                    for k in range(4):
                        dve.wait_ge(outer, it * 4 + (blk * GN + k + 1))
                        for t in range(GT):
                            col = it * (4 * GT) + (blk * GB + k * GT + t)
                            nc.vector.tensor_scalar(b.rows[:, k, t], e.c["iota"], e.rowT[:, bass.ds(col, 1)],
                                                    e.gateT[:, bass.ds(col, 1)], ALU.is_equal, ALU.mult)
                            oh = nc.vector.tensor_scalar(b.cols[:, k, t], e.c["iota"], e.colT[:, bass.ds(col, 1)],
                                                         None, ALU.is_equal)
                        oh.then_inc(hot, 1)

        @block.tensor
        def _(pe):
            pe.sem_inc(outer, 4)
            for blk in range(nblk):
                with pe.Fori(0, GN // 4) as it:
                    for k in range(4):
                        pe.wait_ge(hot, it * 4 + (blk * GN + k + 1))
                        pe.wait_ge(stored, it * 4 + (blk * GN + k + 1))
                        for t in range(GT):
                            mm = nc.tensor.matmul(e.ps[:, k, t * P:(t + 1) * P], b.cols[:, k, t], b.rows[:, k, t])
                        mm.then_inc(outer, 1)

        @block.scalar
        def _(act):
            act.sem_inc(stored, 4)
            for blk in range(nblk):
                if blk >= 2:
                    act.wait_ge(saved[blk % 2], 16 * (blk // 2))
                with act.Fori(0, GN // 4) as it:
                    for k in range(4):
                        act.wait_ge(outer, it * 4 + (blk * GN + k + 5))
                        nc.scalar.activation(
                            b.table[:, blk % 2].rearrange("p i t -> p t i")[:, bass.ds(it * (4 * GT) + k * GT, GT), :],
                            e.ps[:, k, :].rearrange("p (t i) -> p t i", t=GT), ACT.Copy).then_inc(stored, 1)

        @block.sync
        def _(sp):
            for blk in range(nblk):
                sp.wait_ge(stored, GN * (blk + 1) + 4)
                sp.dma_start(e.gtab[blk], b.table[:, blk % 2].rearrange("p i t -> p (i t)")).then_inc(saved[blk % 2], 16)
            for x in range(2):
                sp.wait_ge(saved[x], 16 * (nblk // 2))


def phase_experts(nc, e, nxt, x, b):
    name = "w_u"
    taken, weighed, mixed, added = e.sem("gelu_taken"), e.sem("weighed"), e.sem("mixed"), e.sem("added")
    v_in = [e.sem(f"v_in{p}") for p in range(2)]
    g_in = [e.sem(f"g_in{p}") for p in range(2)]
    base = e.base[name]
    ng = NK // 4
    with nc.Block() as block:
        @block.sync
        def _(sp):
            stream(e, sp, name, nxt)

        @block.gpsimd
        def _(pool):
            with pool.Fori(0, ng // 2) as it:
                for p in range(2):
                    pool.wait_ge(mixed, it * 16 + (8 * p + 8))
                    pool.dma_start(b.v[:, p], e.w["w_pv"][it * 2 + p]).then_inc(v_in[p], 16)
                    src = e.gtab.rearrange("b j n -> j b n")[:, :, bass.ds(it * (8 * GB) + 4 * GB * p, 4 * GB)]
                    pool.dma_start(b.g[:, p].rearrange("p b i t -> p b (i t)"), src).then_inc(g_in[p], 16)

        @block.tensor
        def _(pe):
            pe.sem_inc(mixed, 16)

            def hidden(it, p, d=0):
                for k in range(4):
                    pe.wait_ge(e.slot_full[k], it * 32 + 16 * (base // SLOTS + p + 1))
                    pe.wait_ge(taken, it * 8 + (4 * p + k + 1))
                    for c in range(DC):
                        mm = nc.tensor.matmul(e.ps[:, k, :], e.ring[:, k, c * P:(c + 1) * P], x[:, c, META:L],
                                              start=(c == 0), stop=(c == DC - 1))
                    mm.then_inc(e.tiles_used, 1)

            def mix(it, p):
                pe.wait_ge(v_in[p], it * 16 + 16)
                pe.wait_ge(weighed, it * 8 + (4 * p + 4 + 4))
                for o in range(8):
                    pe.wait_ge(added, it * 16 + (8 * p + o + 1))
                    for i in range(4):
                        mm = nc.tensor.matmul(e.ps[:, 4 + o % 4, :], b.v[:, p, i * D + o * P:i * D + (o + 1) * P],
                                              b.w[:, p, i], start=(i == 0), stop=(i == 3))
                    mm.then_inc(mixed, 1)

            hidden(0, 0)
            with pe.Fori(0, ng // 2 - 1) as it:
                hidden(it, 1)
                mix(it, 0)
                hidden(it, 2)
                mix(it, 1)
            last = ng // 2 - 1
            hidden(last, 1)
            mix(last, 0)
            mix(last, 1)

        @block.scalar
        def _(act):
            act.sem_inc(taken, 4)
            with act.Fori(0, ng) as it:
                for k in range(4):
                    act.wait_ge(e.tiles_used, it * 4 + (base + k + 1))
                    act.wait_ge(weighed, it * 4 + (k + 1))
                    nc.scalar.activation(b.gelu[:, k], e.ps[:, k, :], ACT.Gelu).then_inc(taken, 1)

        @block.vector
        def _(dve):
            dve.sem_inc(added, 4)
            dve.sem_inc(weighed, 4)

            def weigh(it, p, pp=None):
                pp = p if pp is None else pp
                dve.wait_ge(g_in[pp], it * 16 + 16 * (p // 2 + 1))
                dve.wait_ge(mixed, it * 16 + (8 * p + 8))
                for k in range(4):
                    dve.wait_ge(taken, it * 8 + (4 * p + k + 5))
                    blocks = [x.rearrange("p (b t) -> p b t", t=GB) for x in (b.w[:, pp, k], b.gelu[:, k])]
                    nc.vector.tensor_tensor(blocks[0], blocks[1], b.g[:, pp, :, k], ALU.mult).then_inc(weighed, 1)

            def add(it, p):
                for o in range(8):
                    dve.wait_ge(mixed, it * 16 + (8 * p + o + 17))
                    dve.wait_ge(added, it * 16 + (8 * p + 4)) if o == 0 else None
                    nc.vector.tensor_tensor(e.h[:, o, META:L], e.h[:, o, META:L], e.ps[:, 4 + o % 4, :],
                                            ALU.add).then_inc(added, 1)

            weigh(0, 0)
            with dve.Fori(0, ng // 2 - 1) as it:
                weigh(it, 1)
                add(it, 0)
                weigh(it, 2, 0)
                add(it, 1)
            last = ng // 2 - 1
            weigh(last, 1)
            add(last, 0)
            add(last, 1)


def phase_meta2(nc, e):
    s = e.sem("meta2")
    with nc.Block() as block:
        @block.sync
        def _(sp):
            sp.dma_start(e.h[:, :, 0:META], e.w["meta2"]).then_inc(s, 16)
            sp.wait_ge(s, 16)


def phase_ffn_up(nc, e, name, nxt, src, g, tmp):
    a_taken, b_taken = e.sem(f"{name}_a"), e.sem(f"{name}_b")
    base = e.base[name]
    loops = 2 * FT // SLOTS
    with nc.Block() as block:
        @block.sync
        def _(sp):
            stream(e, sp, name, nxt)

        @block.tensor
        def _(pe):
            with pe.Fori(0, loops) as it:
                for k in range(SLOTS):
                    slot_wait(e, pe, name, it, k)
                    pe.wait_ge(b_taken if k % 2 else a_taken, it * 2 + (k // 2 + 1))
                    tile_matmuls(nc, e, k, DC, lambda c, hf: half(src[:, c], hf), 2 * k).then_inc(e.tiles_used, 1)

        @block.scalar
        def _(act):
            act.sem_inc(a_taken, 2)
            with act.Fori(0, loops) as it:
                for j in range(2):
                    act.wait_ge(e.tiles_used, it * SLOTS + (base + 2 * j + 1))
                    act.wait_ge(b_taken, it * 2 + (j + 1))
                    nc.scalar.activation(halves(tmp[:, j]), e.ps[:, 4 * j:4 * j + 2, 0:HL], ACT.Silu).then_inc(a_taken, 1)

        @block.vector
        def _(dve):
            dve.sem_inc(b_taken, 2)
            with dve.Fori(0, loops) as it:
                for j in range(2):
                    dve.wait_ge(e.tiles_used, it * SLOTS + (base + 2 * j + 2))
                    dve.wait_ge(a_taken, it * 2 + (j + 3))
                    nc.vector.tensor_tensor(halves(g[:, it * 2 + j]), e.ps[:, 4 * j + 2:4 * j + 4, 0:HL],
                                            halves(tmp[:, j]), ALU.mult).then_inc(b_taken, 1)


def phase_ffn_down(nc, e, name, nxt, g, y):
    taken = e.sem(f"{name}_taken")
    base = e.base[name]
    nb = FT // 2
    with nc.Block() as block:
        @block.sync
        def _(sp):
            stream(e, sp, name, nxt)

        @block.tensor
        def _(pe):
            with pe.Fori(0, DC // 2) as it:
                for j in range(2):
                    for k in (2 * j, 2 * j + 1):
                        slot_wait(e, pe, name, it, k)
                    pe.wait_ge(taken, it * 2 + (j + 1))
                    for hf in range(2):
                        for c in range(FT):
                            k = 2 * j + c // nb
                            mm = nc.tensor.matmul(e.ps[:, 4 * j + hf, 0:HL], e.ring[:, k, (c % nb) * P:(c % nb + 1) * P],
                                                  half(g[:, c], hf), start=(c == 0), stop=(c == FT - 1))
                    mm.then_inc(e.tiles_used, 2)

        @block.scalar
        def _(act):
            act.sem_inc(taken, 2)
            with act.Fori(0, DC // 2) as it:
                for j in range(2):
                    act.wait_ge(e.tiles_used, it * SLOTS + (base + 2 * j + 2))
                    nc.scalar.activation(halves(y[:, it * 2 + j]), e.ps[:, 4 * j:4 * j + 2, 0:HL],
                                         ACT.Copy).then_inc(taken, 1)


def phase_sconv(nc, e, z):
    w = e.p["sconv"]
    st = [Steps(e.sem(f"sconv{b}"), ["mul", "t1", "t0", "t2", "out"]) for b in range(2)]
    with nc.Block() as block:
        @block.vector
        def _(dve):
            V = nc.vector
            for i0 in (0, 2):
                for name in st[0].names:
                    for i in (i0, i0 + 1):
                        s, x, o = st[i % 2], z[:, 8 + i], e.sq[:, i % 2]
                        s.at(dve, name, i // 2)
                        if name == "mul":
                            ins = V.tensor_tensor(x, x, z[:, 12 + i], ALU.mult)
                        elif name == "t1":
                            ins = V.tensor_scalar(o, x, w[:, 4 + i:5 + i], None, ALU.mult)
                        elif name == "t0":
                            ins = V.scalar_tensor_tensor(out=o[:, 1:L], in0=x[:, 0:L - 1], scalar=w[:, i:i + 1],
                                                         in1=o[:, 1:L], op0=ALU.mult, op1=ALU.add)
                        elif name == "t2":
                            ins = V.scalar_tensor_tensor(out=o[:, 0:L - 1], in0=x[:, 1:L], scalar=w[:, 8 + i:9 + i],
                                                         in1=o[:, 0:L - 1], op0=ALU.mult, op1=ALU.add)
                        else:
                            ins = V.tensor_tensor(z[:, 4 + i], z[:, 4 + i], o, ALU.mult)
                        ins.then_inc(s.sem, 1)


def phase_fourier(nc, e, z, dl, pm):
    loaded, one, one_out = e.sem("dft_in"), e.sem("dft_1"), e.sem("dft_1out")
    two, two_out = e.sem("dft_2"), e.sem("dft_2out")
    items = [(b, i) for b in range(len(TB)) for i in range(4)]
    cs = e.consts[:, CONST_COLS["dft_c"][0]:CONST_COLS["dft_c"][0] + 2 * P]
    with nc.Block() as block:
        @block.sync
        def _(sp):
            sp.dma_start(dl, e.w["dft_l"]).then_inc(loaded, 16)

        @block.tensor
        def _(pe):
            for n, (b, i) in enumerate(items):
                t0, rows = TB[b]
                if n >= 4:
                    pe.wait_ge(one_out, n - 3)
                nc.tensor.matmul(e.ps[0:rows, n % 4, 0:2 * P], z[:, i, t0:t0 + rows], cs).then_inc(one, 1)
            pe.wait_ge(loaded, 16)
            pe.wait_ge(one_out, len(items))
            for i in range(4):
                if i >= 2:
                    pe.wait_ge(two_out, i - 1)
                for hf in range(2):
                    for b, (t0, rows) in enumerate(TB):
                        for s in range(2):
                            mm = nc.tensor.matmul(e.ps[:, 4 + 2 * (i % 2) + hf, 0:HL],
                                                  pm[0:rows, b, i, s * P:(s + 1) * P], half(dl[0:rows, b, s], hf),
                                                  start=(b == 0 and s == 0), stop=(b == len(TB) - 1 and s == 1))
                mm.then_inc(two, 1)

        @block.scalar
        def _(act):
            for n, (b, i) in enumerate(items):
                rows = TB[b][1]
                act.wait_ge(one, n + 1)
                nc.scalar.activation(pm[0:rows, b, i], e.ps[0:rows, n % 4, 0:2 * P], ACT.Copy).then_inc(one_out, 1)
            for i in range(4):
                act.wait_ge(two, i + 1)
                nc.scalar.activation(halves(z[:, i]), e.ps[:, 4 + 2 * (i % 2):6 + 2 * (i % 2), 0:HL],
                                     ACT.Copy).then_inc(two_out, 1)


def phase_gates2(nc, e, src, g):
    st = Steps(e.sem("g2"), ["z", "raw", "alog", "sig", "abs", "exp", "ln", "pos", "sp", "g", "cum", "back", "cols",
                             "evac", "ecol", "nbeta", "nbe"])
    with nc.Block() as block:
        @block.tensor
        def _(pe):
            for hf in range(2):
                for c in range(DC):
                    mm = nc.tensor.matmul(e.ps[0:16, hf, 0:HL], e.wg2[:, c], half(src[:, c], hf),
                                          start=(c == 0), stop=(c == DC - 1))
            mm.then_inc(st.sem, 1)
            st.at(pe, "cols")
            for n in range(NCH):
                t = slice(n * CH, (n + 1) * CH)
                nc.tensor.matmul(e.ps[0:CH, 2, 8 * n:8 * n + 8], g.cum[:, t], e.c["sel_gf"][0:16], start=True, stop=False)
                nc.tensor.matmul(e.ps[0:CH, 2, 8 * n:8 * n + 8], g.back[:, t], e.c["sel_gb"][0:16], start=False, stop=True)
                mm = nc.tensor.matmul(e.ps[0:CH, 3, 8 * n:8 * n + 8], g.beta[:, t], e.c["sel_beta"][0:16])
            mm.then_inc(st.sem, 1)

        @block.scalar
        def _(act):
            A = nc.scalar.activation
            st.at(act, "raw")
            A(halves(g.raw), e.ps[0:16, 0:2, 0:HL], ACT.Identity, bias=e.p["dt"][0:16]).then_inc(st.sem, 1)
            st.at(act, "alog")
            A(g.ea, e.p["alog"][0:16], ACT.Exp).then_inc(st.sem, 1)
            st.at(act, "sig")
            A(g.beta, g.raw, ACT.Sigmoid).then_inc(st.sem, 1)
            st.at(act, "abs")
            A(g.t1, g.raw, ACT.Abs).then_inc(st.sem, 1)
            st.at(act, "exp")
            A(g.t2, g.t1, ACT.Exp, scale=-1.0).then_inc(st.sem, 1)
            st.at(act, "ln")
            A(g.t1, g.t2, ACT.Ln, bias=e.one[0:16]).then_inc(st.sem, 1)
            st.at(act, "ecol")
            A(g.nbe, g.gcol, ACT.Exp).then_inc(st.sem, 1)

        @block.vector
        def _(dve):
            V = nc.vector
            st.at(dve, "pos")
            V.tensor_scalar(g.t2, g.raw, 0.0, None, ALU.max).then_inc(st.sem, 1)
            st.at(dve, "sp")
            V.tensor_tensor(g.t2, g.t2, g.t1, ALU.add).then_inc(st.sem, 1)
            st.at(dve, "g")
            V.tensor_scalar(g.t1, g.t2, g.ea, -1.0, ALU.mult, ALU.mult).then_inc(st.sem, 1)
            st.at(dve, "cum")
            for n in range(NCH):
                t = slice(n * CH, (n + 1) * CH)
                ins = V.tensor_tensor_scan(g.cum[:, t], e.ones_row[0:16, 0:CH], g.t1[:, t], 0.0, ALU.mult, ALU.add)
            ins.then_inc(st.sem, 1)
            st.at(dve, "back")
            for n in range(NCH):
                t = slice(n * CH, (n + 1) * CH)
                ins = V.scalar_tensor_tensor(out=g.back[:, t], in0=g.t1[:, t],
                                             scalar=g.cum[:, (n + 1) * CH - 1:(n + 1) * CH], in1=g.cum[:, t],
                                             op0=ALU.add, op1=ALU.subtract)
            ins.then_inc(st.sem, 1)
            st.at(dve, "evac")
            V.tensor_copy(g.gcol, e.ps[0:CH, 2, 0:8 * NCH])
            V.tensor_copy(g.bcol, e.ps[0:CH, 3, 0:8 * NCH]).then_inc(st.sem, 1)
            st.at(dve, "nbeta")
            V.tensor_scalar(g.nbcol, g.bcol, -1.0, None, ALU.mult).then_inc(st.sem, 1)
            st.at(dve, "nbe")
            V.tensor_tensor(g.nbe, g.nbe, g.nbcol, ALU.mult).then_inc(st.sem, 1)


def phase_deltanet(nc, e, g, z, w):
    names = ["stage", "bc", "ebc", "qd", "args", "exps", "gram", "m1", "m2", "m3", "m4", "tr1", "tre", "kv", "p2", "p2e",
             "p4", "p4e", "z2", "p8", "p8e", "z3", "z4p", "z4", "fw", "fwe", "zte", "f2", "f2e", "f4", "f4e",
             "v1", "v1e", "v2", "v2e", "v3", "v3e", "ks", "r1", "r2", "vn", "vne", "o", "oe", "s1", "s2"]
    st = [Steps(e.sem(f"dn{d}"), names, looped=True) for d in range(2)]
    c = e.c
    q, kk, v = z[:, 16:20], z[:, 20:24], z[:, 24:28]
    edge = [CH - 1, 0]
    mT, mR = [c["below"], c["above"]], [c["strict_f"], c["strict_b"]]

    at = {}

    def locate(eng, it):
        at["t"] = [eng.snap(it * CH), eng.snap(it * -CH + (NCH - 1) * CH)]
        at["c"] = [eng.snap(it * 8), eng.snap(it * -8 + ((NCH - 1) * 8 + 4))]

    def chunk(it, d):
        return bass.ds(at["t"][d], CH)

    def cols(x, it, d):
        return x[:, bass.ds(at["c"][d], 4)]

    def bank(d, j, rows, n):
        return e.ps[0:rows, 4 * d + j, 0:4 * n].rearrange("p (h x) -> p h x", h=4)

    with nc.Block() as block:
        @block.tensor
        def _(pe):
            M, TR = nc.tensor.matmul, nc.tensor.transpose
            idn, id88 = c["ident"], c["ident"][0:CH, 0:CH]

            def heads(f):
                for h in range(DH):
                    mm = f(h)
                return mm

            with pe.Fori(0, NCH) as it:
                locate(pe, it)

                def step(name, f):
                    for d in range(2):
                        st[d].at(pe, name, it)
                        A, B, C = (bank(d, j, CH, CH) for j in range(3))
                        f(d, w[d], A, B, C).then_inc(st[d].sem, 1)

                def s_bc(d, b, A, B, C):
                    rows = (g.cum, g.back)[d]
                    A = bank(d, 0, P, CH)
                    return heads(lambda h: M(A[:, h], c["bc_g"][0:16, (4 * d + h) * P:(4 * d + h + 1) * P],
                                             rows[:, chunk(it, d)]))

                def s_gram(d, b, A, B, C):
                    heads(lambda h: M(B[:, h], b.k[:, h], b.k[:, h]))
                    return heads(lambda h: M(C[:, h], b.k[:, h], q[:, h, chunk(it, d)]))

                def s_tr1(d, b, A, B, C):
                    heads(lambda h: TR(A[:, h], b.b2[:, h], id88))
                    heads(lambda h: TR(B[:, h], b.b0[:, h], id88))
                    kt, vt = bank(d, 2, CH, P), bank(d, 3, CH, P)
                    heads(lambda h: TR(kt[:, h], b.k[:, h], idn))
                    return heads(lambda h: TR(vt[:, h], b.v[:, h], idn))

                def prod(dst, lhsT, rhs):
                    return heads(lambda h: M(dst[:, h], lhsT[:, h], rhs[:, h]))

                step("bc", s_bc)
                step("gram", s_gram)
                step("tr1", s_tr1)
                step("p2", lambda d, b, A, B, C: (prod(A, b.b3, b.b2), prod(B, b.b2, b.b3))[1])
                step("p4", lambda d, b, A, B, C: (prod(A, b.b6, b.b5), prod(B, b.b5, b.b6), prod(C, b.b6, b.z))[2])
                step("p8", lambda d, b, A, B, C: (prod(A, b.b1, b.b2), prod(C, b.b2, b.z))[1])
                step("z4p", lambda d, b, A, B, C: prod(C, b.b3, b.z))
                step("fw", lambda d, b, A, B, C: (prod(A, b.b4, b.z), prod(B, b.z, b.b4),
                                                  heads(lambda h: TR(C[:, h], b.z[:, h], id88)))[2])
                step("f2", lambda d, b, A, B, C: (prod(A, b.b6, b.b5), prod(B, b.b5, b.b6))[1])
                step("f4", lambda d, b, A, B, C: prod(A, b.b2, b.b1))
                step("v1", lambda d, b, A, B, C: prod(C, b.b3, b.b0))
                step("v2", lambda d, b, A, B, C: prod(C, b.b1, b.b0))
                step("v3", lambda d, b, A, B, C: prod(C, b.b5, b.b0))
                step("ks", lambda d, b, A, B, C: prod(bank(d, 0, CH, P), b.k, b.S))
                step("vn", lambda d, b, A, B, C: prod(bank(d, 1, CH, P), b.b0, b.r))

                def s_o(d, b, A, B, C):
                    o, up = bank(d, 2, P, CH), bank(d, 3, P, P)
                    for h in range(DH):
                        M(o[:, h], b.S[:, h], b.qd[:, h], start=True, stop=False)
                        M(o[:, h], b.vn[:, h], b.at[:, h], start=False, stop=True)
                        mm = M(up[:, h], b.kd[:, h], b.vn[:, h])
                    return mm
                step("o", s_o)

        @block.scalar
        def _(act):
            A_ = nc.scalar.activation
            with act.Fori(0, NCH) as it:
                locate(act, it)

                def step(name, f):
                    for d in range(2):
                        st[d].at(act, name, it)
                        A, B, C = (bank(d, j, CH, CH) for j in range(3))
                        f(d, w[d], A, B, C).then_inc(st[d].sem, 1)

                step("ebc", lambda d, b, A, B, C: A_(b.eb, bank(d, 0, P, CH), ACT.Exp))
                step("exps", lambda d, b, A, B, C: (A_(b.et, b.b1, ACT.Exp), A_(b.er, b.b2, ACT.Exp, scale=-1.0))[1])
                step("tre", lambda d, b, A, B, C: (A_(b.b3, A, ACT.Copy), A_(b.b4, B, ACT.Copy))[1])
                step("p2e", lambda d, b, A, B, C: (A_(b.b5, A, ACT.Copy), A_(b.b6, B, ACT.Copy))[1])
                step("p4e", lambda d, b, A, B, C: (A_(b.b1, A, ACT.Copy), A_(b.b2, B, ACT.Copy))[1])
                step("p8e", lambda d, b, A, B, C: A_(b.b3, A, ACT.Copy))
                step("fwe", lambda d, b, A, B, C: (A_(b.b5, A, ACT.Copy), A_(b.b6, B, ACT.Copy))[1])
                step("f2e", lambda d, b, A, B, C: (A_(b.b1, A, ACT.Copy), A_(b.b2, B, ACT.Copy))[1])
                step("f4e", lambda d, b, A, B, C: A_(b.b3, A, ACT.Copy))
                step("vne", lambda d, b, A, B, C: A_(b.vn, bank(d, 1, CH, P), ACT.Copy))
                step("oe", lambda d, b, A, B, C: A_(z[:, 8 + 4 * d:12 + 4 * d, chunk(it, d)], bank(d, 2, P, CH), ACT.Copy))

        @block.vector
        def _(dve):
            V = nc.vector
            TT = V.tensor_tensor
            for d in range(2):
                V.memset(w[d].S, 0.0).then_inc(st[d].sem, 1)

            def over(x, n):
                return x.unsqueeze(2).broadcast_to([x.shape[0], 4, n])

            def mask(m):
                return m[0:CH, 0:CH].unsqueeze(1).broadcast_to([CH, 4, CH])

            with dve.Fori(0, NCH) as it:
                locate(dve, it)

                def step(name, f):
                    for d in range(2):
                        st[d].at(dve, name, it)
                        A, B, C = (bank(d, j, CH, CH) for j in range(3))
                        f(d, w[d], A, B, C).then_inc(st[d].sem, 1)

                step("stage", lambda d, b, A, B, C: (V.tensor_copy(b.k, kk[:, :, chunk(it, d)]),
                                                     V.tensor_copy(b.v, v[:, :, chunk(it, d)]))[1])
                step("qd", lambda d, b, A, B, C: (TT(b.qd, q[:, :, chunk(it, d)], b.eb, ALU.mult),
                                                  TT(b.b0, A, over(cols(g.gcol, it, d), CH), ALU.subtract))[1])
                step("args", lambda d, b, A, B, C: (TT(b.b1, b.b0, mask(mT[d]), ALU.add),
                                                    TT(b.b2, b.b0, mask(mR[d]), ALU.add))[1])
                step("m1", lambda d, b, A, B, C: (TT(b.at, C, b.et, ALU.mult), TT(b.b0, B, b.er, ALU.mult))[1])
                step("m2", lambda d, b, A, B, C: TT(b.b1, b.b0, over(cols(g.nbcol, it, d), CH), ALU.mult))
                step("m3", lambda d, b, A, B, C: TT(b.b2, b.b1, mask(c["sub"]), ALU.mult))
                step("m4", lambda d, b, A, B, C: (TT(b.b0, b.b1, b.b2, ALU.subtract),
                                                  TT(b.z, b.b2, mask(c["ident"]), ALU.add))[1])
                step("kv", lambda d, b, A, B, C: (
                    TT(b.kd, bank(d, 2, CH, P), over(b.et[:, :, edge[d]], P), ALU.mult),
                    TT(b.vb, bank(d, 3, CH, P), over(cols(g.bcol, it, d), P), ALU.mult))[1])
                for name in ("z2", "z3", "z4"):
                    step(name, lambda d, b, A, B, C: TT(b.z, b.z, C, ALU.add))
                step("zte", lambda d, b, A, B, C: V.tensor_copy(b.b0, C))
                for name in ("v1e", "v2e", "v3e"):
                    step(name, lambda d, b, A, B, C: TT(b.b0, b.b0, C, ALU.add))
                step("r1", lambda d, b, A, B, C: TT(b.r, bank(d, 0, CH, P), over(cols(g.nbe, it, d), P), ALU.mult))
                step("r2", lambda d, b, A, B, C: TT(b.r, b.r, b.vb, ALU.add))
                step("s1", lambda d, b, A, B, C: TT(b.S, b.S, over(b.eb[:, :, edge[d]], P), ALU.mult))
                step("s2", lambda d, b, A, B, C: TT(b.S, b.S, bank(d, 3, P, P), ALU.add))


def phase_dn_sum(nc, e, z):
    with nc.Block() as block:
        @block.vector
        def _(dve):
            nc.vector.tensor_tensor(z[:, 8:12], z[:, 8:12], z[:, 12:16], ALU.add)

        @block.scalar
        def _(act):
            nc.scalar.activation(z[:, 28:32], z[:, 28:32], ACT.Silu)


def phase_merge(nc, e, nxt, src, z, out, tmp):
    name = "w_merge"
    gate_taken, done = e.sem("mg_gate"), e.sem("mg_done")
    base = e.base[name]
    per = DC // SLOTS
    prod = e.sem("mg_prod")
    with nc.Block() as block:
        @block.sync
        def _(sp):
            stream(e, sp, name, nxt)

        @block.tensor
        def _(pe):
            for br in range(3):
                with pe.Fori(0, per) as it:
                    for k in range(SLOTS):
                        pe.wait_ge(e.slot_full[k], it * 16 + 16 * (base // SLOTS + br * per + 1))
                        pe.wait_ge(done, it * SLOTS + (br * DC + k + 1))
                        tile_matmuls(nc, e, k, DC, lambda c, hf: half(src[:, c], hf), 4 * (k % 2))
                        tile_matmuls(nc, e, k, 4, lambda c, hf: half(z[:, 4 * br + c], hf), 4 * (k % 2) + 2,
                                     off=DC).then_inc(e.tiles_used, 1)

        @block.scalar
        def _(act):
            for br in range(3):
                with act.Fori(0, per) as it:
                    for k in range(SLOTS):
                        act.wait_ge(e.tiles_used, it * SLOTS + (base + br * DC + k + 1))
                        act.wait_ge(done, it * SLOTS + (br * DC + k + 1))
                        nc.scalar.activation(halves(tmp[:, k % 2]), e.ps[:, 4 * (k % 2):4 * (k % 2) + 2, 0:HL],
                                             ACT.Sigmoid).then_inc(gate_taken, 1)

        @block.vector
        def _(dve):
            dve.sem_inc(done, 2)
            for br in range(3):
                with dve.Fori(0, per) as it:
                    for k in range(SLOTS):
                        dve.wait_ge(gate_taken, it * SLOTS + (br * DC + k + 1))
                        y = e.ps[:, 4 * (k % 2) + 2:4 * (k % 2) + 4, 0:HL]
                        o = out[:, it * SLOTS + k]
                        if br == 0:
                            nc.vector.tensor_tensor(halves(o), halves(tmp[:, k % 2]), y, ALU.mult).then_inc(done, 1)
                        else:
                            nc.vector.tensor_tensor(halves(tmp[:, k % 2]), halves(tmp[:, k % 2]), y,
                                                    ALU.mult).then_inc(prod, 1)
                            dve.wait_ge(prod, it * SLOTS + ((br - 1) * DC + k + 1))
                            nc.vector.tensor_tensor(o, o, tmp[:, k % 2], ALU.add).then_inc(done, 1)


STREAMS = [("w_qk", 20, 8), ("w_v", 8, 8), ("w_out", 8, 8), ("w_pq", 16, 8), ("w_u", NK, 8), ("f1_up", 2 * FT, 8),
           ("f1_down", 16, 11), ("w_mix", 32, 8), ("w_merge", 24, 12), ("w_out2", 8, 8), ("f2_up", 2 * FT, 8),
           ("f2_down", 16, 11)]


class Arena:

    def __init__(self, region, at=0):
        self.region, self.n = region, at

    def take(self, *shape, rows=P):
        size = int(np.prod(shape))
        ap = self.region[0:rows, self.n:self.n + size]
        self.n += size
        assert self.n <= self.region.shape[1], (self.n, self.region.shape)
        names = "abcd"[:len(shape)]
        if len(shape) > 1:
            ap = ap.rearrange(f"p ({' '.join(names)}) -> p {' '.join(names)}", **dict(zip(names[1:], shape[1:])))
        return ap


def phase_load(nc, e, pool_consts):
    s = e.sem("loaded")
    with nc.Block() as block:
        @block.sync
        def _(sp):
            loads = [(e.h, e.w["h0"]), (e.consts, e.w["consts"]), (e.params, e.w["params"]),
                     (e.wg1, e.w["wg1"]), (e.wg2, e.w["wg2"])]
            for dst, src in loads:
                sp.dma_start(dst, src).then_inc(s, 16)
            prefetch(e, sp, STREAMS[0][0], 0)
            sp.wait_ge(s, 16 * len(loads))

        @block.vector
        def _(dve):
            nc.vector.memset(e.eps, EPS)
            nc.vector.memset(e.one, 1.0)
            nc.vector.memset(e.zero, 0.0)


def hybrid_kernel(nc, w, out, stop=None):
    with ExitStack() as ctx:
        e = Env()
        e.w, e.sems = w, {}

        def sem(name):
            e.sems[name] = ctx.enter_context(nc.semaphore(name))
            return e.sems[name]

        def sb(name, *shape, dt=F32):
            return ctx.enter_context(nc.sbuf_tensor(name, [P, *shape], dt))[:]

        e.sem = sem
        e.h, e.hn = sb("h", DC, L), sb("hn", DC, L)
        e.ring = sb("ring", SLOTS, SLOT)
        e.consts, e.params = sb("const_tab", NCONST), sb("param_tab", NPARAM)
        e.wg1, e.wg2 = sb("wg1_sb", DC, 16), sb("wg2_sb", DC, 16)
        scratch = sb("scratch", 6 * L)
        misc = sb("misc", 4)
        e.sq = scratch[:, 0:4 * L].rearrange("p (b t) -> p b t", b=4)
        e.r0, e.r1 = scratch[:, 4 * L:5 * L], scratch[:, 5 * L:6 * L]
        e.eps, e.one, e.zero = misc[:, 0:1], misc[:, 1:2], misc[:, 2:3]
        e.ones_row, e.zero_row = e.one.broadcast_to([P, L]), e.zero.broadcast_to([P, L])
        left = (nc.sbuf_bytes_remaining - 64) // 4
        region = sb("arena", left)
        ps = ctx.enter_context(nc.psum_tensor("ps", [P, 8, WIDE], F32))
        e.ps = ps[:]
        e.psf = e.ps.rearrange("p b n -> p (b n)")
        e.c = {k: e.consts[:, a:a + n] for k, (a, n) in CONST_COLS.items()}
        e.p = {k: e.params[:, a:a + n] for k, (a, n) in PARAM_COLS.items()}
        e.tiles_used = sem("tiles_used")
        e.slot_full = [sem(f"slot_full{k}") for k in range(SLOTS)]
        e.base, nxt = {}, {}
        at = 0
        for i, (name, n, _) in enumerate(STREAMS):
            e.base[name] = at
            at += n
            nxt[name] = STREAMS[i + 1][0] if i + 1 < len(STREAMS) else None
        e.gtab = nc.dram_tensor("gate_table", (T // GB, P, NK * GB), F32).ap()

        def finish(src):
            s = sem("out_saved")
            with nc.Block() as block:
                @block.sync
                def _(sp):
                    sp.dma_start(out, src).then_inc(s, 16)
                    sp.wait_ge(s, 16)

        phase_load(nc, e, None)

        a = Arena(region)
        z = a.take(20, L)
        vt = a.take(len(TB), D)
        qz = a.take(FH, L)
        yt = a.take(len(TB), 4 * P)
        e.fp = a.take(2, L)
        e.fpT = a.take(2, len(TB), P)
        e.fmx = a.take(2, 4)
        e.et, e.pt, e.dg = a.take(L), a.take(L), a.take(L)
        g = Env()
        g.raw, g.t1, g.t2, g.cum = (a.take(L, rows=16) for _ in range(4))
        g.rmax = a.take(L, rows=4)
        g.acol = a.take(len(TB), 4)
        phase_norm(nc, e, "n1", e.h, e.p["norm_mix"], e.hn)
        phase_linear(nc, e, "w_qk", nxt["w_qk"], e.hn, 20, ("act", lambda it, k, s: nc.scalar.activation(
            halves(z[:, it * SLOTS + k]), s, ACT.Copy)))
        phase_values(nc, e, nxt["w_v"], e.hn, vt)
        phase_gates1(nc, e, e.hn, g)
        cw = e.p["conv1"]
        phase_conv_silu(nc, e, "conv1", [z[:, i] for i in range(8)],
                        [[(0, cw[:, 24 + i:25 + i]), (-1, cw[:, 16 + i:17 + i]), (-2, cw[:, 8 + i:9 + i]),
                          (-3, cw[:, i:i + 1])] for i in range(8)])
        half_gain = [e.params[:, PARAM_COLS["fq"][0] + j:PARAM_COLS["fq"][0] + j + 1] for j in range(2)]
        phase_head_norm(nc, e, "fqk", [z[:, i] for i in range(8, 16)], e.c["halves"], 1.0 / FD,
                        [half_gain] * 4 + [[e.p["fk"]]] * 4,
                        outs=[[qz[:, 2 * i], qz[:, 2 * i + 1]] for i in range(4)] + [[z[:, 12 + i]] for i in range(4)])
        phase_mlstm(nc, e, g, z[:, 0:4], z[:, 4:8], vt, z[:, 0:4])
        phase_sigmoid(nc, e, "mo", z[:, 16:20])
        phase_head_norm(nc, e, "mout", [z[:, i] for i in range(4)], e.c["ones"], 1.0 / P,
                        [[e.p["m_out"][:, i:i + 1]] for i in range(4)], mul=[z[:, 16 + i] for i in range(4)])
        phase_fox(nc, e, g, qz, z[:, 12:16], vt, yt, z[:, 4:8])
        if stop == "y1":
            return finish(z[:, 0:8, META:L])
        phase_linear(nc, e, "w_out", nxt["w_out"], z[:, 0:8], 8, ("dve", lambda it, k, s: nc.vector.tensor_tensor(
            halves(e.h[:, it * SLOTS + k]), s, halves(e.h[:, it * SLOTS + k]), ALU.add)))
        if stop == "h1":
            return finish(e.h[:, :, META:L])

        a = Arena(region)
        e.rowT, e.colT, e.gateT = a.take(T), a.take(T), a.take(T)
        mark = a.n
        qT = a.take(2 * PH, L)
        keys = a.take(2 * PH, NK)
        kb = []
        for _ in range(2):
            b = Env()
            b.sc = a.take(2 * PH, NK)
            b.val, b.idxf = a.take(2 * PH, TOPK), a.take(2 * PH, TOPK)
            b.idx = a.take(2 * PH, TOPK).bitcast(U32)
            b.top, b.hif, b.lof, b.gate, b.row, b.col = (a.take(PH, TOPK) for _ in range(6))
            b.pos, b.hi, b.lo = (a.take(PH, TOPK).bitcast(U32) for _ in range(3))
            b.tot, b.rec = a.take(PH), a.take(PH)
            kb.append(b)
        phase_norm(nc, e, "n2", e.h, e.p["norm_ffn"], e.hn)
        phase_keys(nc, e, keys)
        phase_linear(nc, e, "w_pq", nxt["w_pq"], e.hn, 16, ("act", lambda it, k, s: nc.scalar.activation(
            halves(qT[:, it * SLOTS + k]), s, ACT.Copy)))
        phase_topk(nc, e, qT[:, :, META:L], keys, kb)
        a = Arena(region, mark)
        b = Env()
        b.rows, b.cols = a.take(4, GT, P), a.take(4, GT, P)
        b.table = a.take(2, NK, GB)
        phase_gate_table(nc, e, b)
        a = Arena(region)
        b = Env()
        b.v = a.take(2, 4 * D)
        b.g = a.take(2, T // GB, 4, GB)
        b.gelu = a.take(4, T)
        b.w = a.take(2, 4, T)
        phase_experts(nc, e, nxt["w_u"], e.hn, b)
        if stop == "h2":
            return finish(e.h[:, :, META:L])

        phase_meta2(nc, e)
        gain = e.p["gains2"]

        def ffn(n, name):
            a = Arena(region)
            gg, tmp, y = a.take(FT, L), a.take(2, L), a.take(DC, L)
            phase_norm(nc, e, f"{name}a", e.h, gain[:, 8 * n:8 * n + 8], e.hn)
            phase_ffn_up(nc, e, name + "_up", nxt[name + "_up"], e.hn, gg, tmp)
            phase_ffn_down(nc, e, name + "_down", nxt[name + "_down"], gg, y)
            phase_norm(nc, e, f"{name}b", y, gain[:, 8 * n + 8:8 * n + 16], y, tail=0.5)

        ffn(0, "f1")
        if stop == "h3":
            return finish(e.h[:, :, META:L])
        a = Arena(region)
        z = a.take(32, L)
        phase_norm(nc, e, "n3", e.h, gain[:, 16:24], e.hn)
        phase_linear(nc, e, "w_mix", nxt["w_mix"], e.hn, 32, ("act", lambda it, k, s: nc.scalar.activation(
            halves(z[:, it * SLOTS + k]), s, ACT.Copy)))
        mark = a.n
        dl, pm = a.take(len(TB), 2, L), a.take(len(TB), 4, 2 * P)
        phase_fourier(nc, e, z, dl, pm)
        phase_sconv(nc, e, z)
        cw = e.p["dnconv"]
        phase_conv_silu(nc, e, "conv2", [z[:, 16 + i] for i in range(12)],
                        [[(0, cw[:, 12 + i:13 + i]), (-1, cw[:, i:i + 1]), (1, cw[:, 24 + i:25 + i])]
                         for i in range(12)])
        phase_head_norm(nc, e, "dnqk", [z[:, 16 + i] for i in range(8)], e.c["ones"], 1.0,
                        [[float(P) ** -0.5]] * 4 + [[1.0]] * 4)
        a = Arena(region, mark)
        g = Env()
        g.cum, g.back = a.take(L, rows=16), a.take(L, rows=16)
        g.gcol, g.bcol, g.nbcol, g.nbe = (a.take(8 * NCH, rows=CH) for _ in range(4))
        g.ea = misc[0:16, 3:4]
        g.raw, g.t1, g.t2, g.beta = (e.sq[0:16, i] for i in range(4))
        phase_gates2(nc, e, e.hn, g)
        dw = []
        for _ in range(2):
            b = Env()
            big = [a.take(4, CH) for _ in range(4)]
            b.k, b.eb, b.qd, full = big
            b.v, b.b3 = full, full[0:CH]
            b.et, b.at, b.z, b.b0, b.b4 = (a.take(4, CH, rows=CH) for _ in range(5))
            n = a.n
            b.b1, b.b2 = a.take(4, CH, rows=CH), a.take(4, CH, rows=CH)
            b.vn = Arena(region, n).take(4, P, rows=CH)
            n = a.n
            b.b5, b.b6 = a.take(4, CH, rows=CH), a.take(4, CH, rows=CH)
            b.r = Arena(region, n).take(4, P, rows=CH)
            b.er = b.z
            b.vb, b.kd = a.take(4, P, rows=CH), a.take(4, P, rows=CH)
            b.S = a.take(4, P)
            dw.append(b)
        phase_deltanet(nc, e, g, z, dw)
        phase_dn_sum(nc, e, z)
        phase_head_norm(nc, e, "dno", [z[:, 8 + i] for i in range(4)], e.c["ones"], 1.0 / P, [[e.p["dn"]]] * 4,
                        mul=[z[:, 28 + i] for i in range(4)])
        if stop == "z3":
            return finish(z[:, 4:12, META:L])
        a = Arena(region, mark)
        merged, tmp, y = a.take(DC, L), a.take(2, L), a.take(DC, L)
        phase_merge(nc, e, nxt["w_merge"], e.hn, z, merged, tmp)
        phase_linear(nc, e, "w_out2", nxt["w_out2"], merged, 8, ("act", lambda it, k, s: nc.scalar.activation(
            halves(y[:, it * SLOTS + k]), s, ACT.Copy)))
        phase_norm(nc, e, "n4", y, gain[:, 24:32], y, tail=1.0)
        if stop == "h4":
            return finish(e.h[:, :, META:L])
        ffn(4, "f2")
        finish(e.h[:, :, META:L])


def phase_sigmoid(nc, e, tag, x):
    with nc.Block() as block:
        @block.scalar
        def _(act):
            nc.scalar.activation(x, x, ACT.Sigmoid)


def phase_keys(nc, e, keys):
    s = e.sem("keys_in")
    with nc.Block() as block:
        @block.sync
        def _(sp):
            sp.dma_start(keys, e.w["keys"]).then_inc(s, 16)
            sp.wait_ge(s, 16)


def lay_out(inputs):
    x = {k: np.asarray(v) for k, v in inputs.items()}
    f = np.float32

    def cols(v):
        return v.reshape(-1, P).T

    def tiles(w):
        k, n = w.shape
        return w.reshape(k // P, P, n // P, P).transpose(2, 1, 0, 3).reshape(n // P, P, k)

    def token_T(h):
        return h.T.reshape(DC, P, -1).transpose(1, 0, 2)

    def rows16(parts):
        v = np.zeros((P, 1), f)
        for at, p in parts:
            v[at:at + p.size, 0] = p.ravel()
        return v

    a = {}
    a["h0"] = token_T(np.concatenate([x["meta_tokens"], x["x"][0]], 0))
    a["meta2"] = token_T(x["meta_tokens_2"])
    w1 = x["w_in"][0]
    mq, mk, mv, mo, mi, mf, fq, fk, fv, ff = np.split(w1, np.cumsum([512, 512, 512, 512, 4, 4, 512, 512, 512])[:9], 1)
    a["w_qk"] = tiles(np.concatenate([mq, mk, fq, fk, mo], 1))
    a["w_v"] = tiles(np.concatenate([mv, fv], 1))
    a["wg1"] = np.concatenate([mi, mf, ff], 1).reshape(DC, P, 16).transpose(1, 0, 2)
    a["w_out"] = tiles(x["w_out"][0])
    a["w_pq"] = tiles(x["peer_query"][0])
    a["keys"] = x["peer_sub_keys"][0].reshape(2 * PH, NK, P).transpose(2, 0, 1)
    a["w_u"] = x["peer_u"][0].reshape(NK, NK, DC, P).transpose(0, 3, 2, 1).reshape(NK, P, D)
    a["w_pv"] = x["peer_v"][0].reshape(NK // 4, 4, NK, D).transpose(0, 2, 1, 3).reshape(NK // 4, NK, 4 * D)
    for n in (1, 2):
        wi, wo = x[f"ffn{n}_wi_2"][0], x[f"ffn{n}_wo_2"][0]
        up = np.stack([tiles(wi[:, :FF]), tiles(wi[:, FF:])], 1)
        a[f"f{n}_up"] = up.reshape(2 * FT, P, D)
        down = tiles(wo).reshape(DC, P, 2, FF // 2).transpose(0, 2, 1, 3)
        a[f"f{n}_down"] = down.reshape(2 * DC, P, FF // 2)
    w2 = x["w_in_2"][0]
    uf, sc, qkv, zz, bl, al, gl = np.split(w2, np.cumsum([512, 1536, 1536, 512, 8, 8])[:6], 1)
    a["w_mix"] = tiles(np.concatenate([uf, sc, qkv, zz], 1))
    a["wg2"] = np.concatenate([bl, al], 1).reshape(DC, P, 16).transpose(1, 0, 2)
    outs = np.concatenate([tiles(x[k][0]) for k in ("w_fourier_2", "w_sconv_out_2", "w_dn_out_2")], 0)
    a["w_merge"] = np.concatenate([tiles(gl), outs], 2)
    a["w_out2"] = tiles(x["w_out_2"][0])
    consts = const_tables()
    a["consts"] = np.concatenate([consts[k][:, :n] for k, (_, n) in CONST_COLS.items()], 1)
    t = np.arange(L)
    ang = 2 * np.pi * (np.outer(t, t) % L) / L
    dl = np.zeros((len(TB) * P, 2, L), f)
    dl[:L, 0], dl[:L, 1] = np.cos(ang) / np.sqrt(L), -np.sin(ang) / np.sqrt(L)
    a["dft_l"] = dl.reshape(len(TB), P, 2, L).transpose(1, 0, 2, 3)
    z64 = np.zeros((FD, 1), f)
    gq, gk = x["f_q_norm"][0].reshape(FD, 1), x["f_k_norm"][0].reshape(FD, 1)
    par = {
        "norm_mix": cols(x["norm_mix"][0]), "norm_ffn": cols(x["norm_ffn"][0]),
        "gains2": np.concatenate([cols(v) for v in x["norm_gains_2"][0]], 1),
        "conv1": np.concatenate([cols(v) for v in x["conv_qk"][0]], 1), "m_out": cols(x["m_out_norm"][0]),
        "fq": np.concatenate([np.concatenate([gq, z64], 0), np.concatenate([z64, gq], 0)], 1),
        "fk": np.concatenate([gk, gk], 0),
        "bias1": rows16([(0, x["b_igate"]), (4, x["b_fgate_m"]), (8, x["b_fgate_f"])]),
        "sconv": np.concatenate([cols(v) for v in x["sconv_w_2"][0]], 1),
        "dnconv": np.concatenate([cols(v) for v in x["dn_conv_w_2"][0]], 1),
        "alog": rows16([(8, x["dn_A_log_2"])]), "dt": rows16([(8, x["dn_dt_bias_2"])]), "dn": cols(x["dn_norm_2"][0]),
    }
    a["params"] = np.concatenate([par[k] for k in PARAM_COLS], 1)
    return {k: np.ascontiguousarray(v, dtype=f) for k, v in a.items()}


STOP = None


def kernel(**inputs):
    import concourse.bacc as bacc
    from concourse.bass_utils import run_bass_kernel_spmd as run

    nc = bacc.Bacc("TRN2", target_bir_lowering=False, num_devices=1)
    arrays = {f"in_{k}": v for k, v in lay_out(inputs).items()}
    w = {k[3:]: nc.dram_tensor(k, v.shape, F32, kind="ExternalInput").ap() for k, v in arrays.items()}
    out = nc.dram_tensor("out_h", (P, DC, T), F32, kind="ExternalOutput").ap()
    hybrid_kernel(nc, w, out, STOP)
    r = run(nc, [arrays], core_ids=[0]).results[0]["out_h"]
    return np.ascontiguousarray(r.transpose(2, 1, 0).reshape(1, T, D))
```
